# Optimizing a Trainium2 kernel written in Bass

```python
import jax, jax.numpy as jnp
from jax import lax
import numpy as np

D_MODEL = 1024
BATCH = 1
SEQ = 512
DEPTH = 1
DEC_BATCH = 1
DEC_SEQ = 32
PAST_LEN = 512

CHUNK = 64
N_HEADS = 16
Q_LORA = 256
KV_LORA = 128
NOPE_DIM = 64
ROPE_DIM = 32
V_DIM = 64
QK_DIM = NOPE_DIM + ROPE_DIM
ROPE_THETA = 10000.0
Q_BLOCK = 128
LRU_WIDTH = D_MODEL
LRU_BLOCKS = 8
LRU_BLOCK_W = LRU_WIDTH // LRU_BLOCKS
LRU_CONV_W = 4
RG_C = 8.0
D_FF = 2816
FFN_CONV_W = 3
EPS = 1e-6
N_IN = Q_LORA + KV_LORA + ROPE_DIM + LRU_WIDTH + 2 * D_MODEL
IN_SPLITS = (Q_LORA,
             Q_LORA + KV_LORA,
             Q_LORA + KV_LORA + ROPE_DIM,
             Q_LORA + KV_LORA + ROPE_DIM + LRU_WIDTH,
             Q_LORA + KV_LORA + ROPE_DIM + LRU_WIDTH + D_MODEL)

kernel_name = 'hybrid_mla_rglru_convffn_stream_step'

def rms_norm(x, g):
    xf = x.astype(jnp.float32)
    y = xf * lax.rsqrt(jnp.mean(xf * xf, axis=-1, keepdims=True) + EPS)
    return (y * g.astype(jnp.float32)).astype(x.dtype)

def rope_tables(pos):
    inv = ROPE_THETA ** (-jnp.arange(0, ROPE_DIM, 2, dtype=jnp.float32) / ROPE_DIM)
    ang = pos.astype(jnp.float32)[:, None] * inv[None, :]
    return jnp.cos(ang), jnp.sin(ang)

def apply_rope(x, cos, sin):
    half = x.shape[-1] // 2
    x1, x2 = x[..., :half], x[..., half:]
    c = cos.astype(x.dtype)
    s = sin.astype(x.dtype)
    return jnp.concatenate([x1 * c - x2 * s, x1 * s + x2 * c], axis=-1)

def causal_dwconv(x, buf, w, b):
    width = w.shape[0]
    t = x.shape[1]
    xc = jnp.concatenate([buf.astype(x.dtype), x], axis=1)
    y = xc[:, 0:t] * w[0]
    for j in range(1, width):
        y = y + xc[:, j:j + t] * w[j]
    return y + b, xc[:, xc.shape[1] - (width - 1):]

def chunk_causal_mla(q_nope, q_rope, k_nope, k_rope, v, q_pos, k_pos):
    b, t, h, _ = q_nope.shape
    qb = t if t <= Q_BLOCK else Q_BLOCK
    nb = t // qb
    scale = QK_DIM ** -0.5
    k_chunk = k_pos // CHUNK

    def to_blocks(a):
        return jnp.moveaxis(a.reshape((b, nb, qb) + a.shape[2:]), 1, 0)

    def one_block(args):
        qn, qr, qp = args
        s = (jnp.einsum('bqhd,bkhd->bhqk', qn, k_nope, preferred_element_type=jnp.float32)
             + jnp.einsum('bqhr,bkr->bhqk', qr, k_rope, preferred_element_type=jnp.float32))
        visible = k_chunk[None, :] <= (qp // CHUNK)[:, None]
        s = jnp.where(visible[None, None], s * scale, -jnp.inf)
        p = jax.nn.softmax(s, axis=-1).astype(v.dtype)
        return jnp.einsum('bhqk,bkhd->bqhd', p, v)

    o = lax.map(one_block, (to_blocks(q_nope), to_blocks(q_rope), q_pos.reshape(nb, qb)))
    return jnp.moveaxis(o, 0, 1).reshape(b, t, h * v.shape[-1])

def rg_lru(u, h0, w_rg, b_rg, w_ig, b_ig, lam):
    b, t, c = u.shape
    ub = u.reshape(b, t, LRU_BLOCKS, LRU_BLOCK_W)
    r = jax.nn.sigmoid(jnp.einsum('btnc,ncd->btnd', ub, w_rg).reshape(b, t, c) + b_rg)
    i = jax.nn.sigmoid(jnp.einsum('btnc,ncd->btnd', ub, w_ig).reshape(b, t, c) + b_ig)
    log_a = (-RG_C * r.astype(jnp.float32)) * jax.nn.softplus(-lam.astype(jnp.float32))
    a = jnp.exp(log_a)
    mult = jnp.sqrt(-jnp.expm1(2.0 * log_a))
    bt = mult * (i * u).astype(jnp.float32)
    bt = bt.at[:, 0].add(a[:, 0] * h0.astype(jnp.float32))

    def combine(left, right):
        a_l, b_l = left
        a_r, b_r = right
        return a_l * a_r, a_r * b_l + b_r

    _, h = lax.associative_scan(combine, (a, bt), axis=1)
    return h.astype(u.dtype), h[:, -1].astype(h0.dtype)

def hybrid_layer(x, q_pos, past_lat, past_kr, h0, lru_buf, ffn_buf,
                 g_mix_norm, w_in, g_q_a, w_q_b, g_kv_a, w_kv_b, g_qn, g_qr, g_kn, g_kr,
                 lru_conv_w, lru_conv_b, w_rg, b_rg, w_ig, b_ig, lru_lambda,
                 w_out, g_ffn_norm, w_up, ffn_conv_w, ffn_conv_b, w_down):
    b, t, _ = x.shape
    xn = rms_norm(x, g_mix_norm)
    z = xn @ w_in
    c_q, c_kv, k_r, u, gate_a, gate_b = jnp.split(z, IN_SPLITS, axis=-1)
    cos, sin = rope_tables(q_pos)
    q = (rms_norm(c_q, g_q_a) @ w_q_b).reshape(b, t, N_HEADS, QK_DIM)
    q_nope = rms_norm(q[..., :NOPE_DIM], g_qn)
    q_rope = apply_rope(rms_norm(q[..., NOPE_DIM:], g_qr), cos[:, None, :], sin[:, None, :])
    c_kv = rms_norm(c_kv, g_kv_a)
    k_r = apply_rope(rms_norm(k_r, g_kr), cos, sin)
    lat_all = jnp.concatenate([past_lat.astype(x.dtype), c_kv], axis=1)
    kr_all = jnp.concatenate([past_kr.astype(x.dtype), k_r], axis=1)
    n_k = lat_all.shape[1]
    kv = (lat_all @ w_kv_b).reshape(b, n_k, N_HEADS, NOPE_DIM + V_DIM)
    k_nope = rms_norm(kv[..., :NOPE_DIM], g_kn)
    v = kv[..., NOPE_DIM:]
    attn = chunk_causal_mla(q_nope, q_rope, k_nope, kr_all, v, q_pos,
                            jnp.arange(n_k, dtype=jnp.int32))
    u_c, lru_buf_new = causal_dwconv(u, lru_buf, lru_conv_w, lru_conv_b)
    rec, h_last = rg_lru(u_c, h0, w_rg, b_rg, w_ig, b_ig, lru_lambda)
    mixed = jax.nn.sigmoid(gate_a) * attn + jax.nn.sigmoid(gate_b) * rec
    x = x + mixed @ w_out
    up = rms_norm(x, g_ffn_norm) @ w_up
    up_c, ffn_buf_new = causal_dwconv(up, ffn_buf, ffn_conv_w, ffn_conv_b)
    gate, val = jnp.split(up_c, 2, axis=-1)
    x = x + (jax.nn.silu(gate) * val) @ w_down
    return x, (c_kv, k_r, h_last, lru_buf_new, ffn_buf_new)

def setup_inputs(seed: int = 0) -> dict:
    key = jax.random.key(seed)
    ks = jax.random.split(key, 40)
    f32 = jnp.float32

    def nrm(k, shape, scale):
        return jax.random.normal(k, shape, f32) * scale

    def gain(k, shape):
        return 1.0 + 0.01 * jax.random.normal(k, shape, f32)

    a0 = jax.random.uniform(ks[29], (DEPTH, LRU_WIDTH), f32, minval=0.9, maxval=0.999)
    return {
        'x_prompt': nrm(ks[0], (BATCH, SEQ, D_MODEL), 1.0),
        'x_sample': nrm(ks[1], (DEC_BATCH, DEC_SEQ, D_MODEL), 1.0),
        'cache_kv_latent': nrm(ks[2], (DEPTH, DEC_BATCH, PAST_LEN, KV_LORA), 1.0),
        'cache_k_rope': nrm(ks[3], (DEPTH, DEC_BATCH, PAST_LEN, ROPE_DIM), 1.0),
        'state_lru_h': nrm(ks[4], (DEPTH, DEC_BATCH, LRU_WIDTH), 0.5),
        'state_lru_conv': nrm(ks[5], (DEPTH, DEC_BATCH, LRU_CONV_W - 1, LRU_WIDTH), 1.0),
        'state_ffn_conv': nrm(ks[6], (DEPTH, DEC_BATCH, FFN_CONV_W - 1, 2 * D_FF), 1.0),
        'g_mix_norm': gain(ks[7], (DEPTH, D_MODEL)),
        'w_in': nrm(ks[8], (DEPTH, D_MODEL, N_IN), D_MODEL ** -0.5),
        'g_q_a': gain(ks[9], (DEPTH, Q_LORA)),
        'w_q_b': nrm(ks[10], (DEPTH, Q_LORA, N_HEADS * QK_DIM), Q_LORA ** -0.5),
        'g_kv_a': gain(ks[11], (DEPTH, KV_LORA)),
        'w_kv_b': nrm(ks[12], (DEPTH, KV_LORA, N_HEADS * (NOPE_DIM + V_DIM)), KV_LORA ** -0.5),
        'g_qn': gain(ks[13], (DEPTH, NOPE_DIM)),
        'g_qr': gain(ks[14], (DEPTH, ROPE_DIM)),
        'g_kn': gain(ks[15], (DEPTH, NOPE_DIM)),
        'g_kr': gain(ks[16], (DEPTH, ROPE_DIM)),
        'lru_conv_w': nrm(ks[17], (DEPTH, LRU_CONV_W, LRU_WIDTH), LRU_CONV_W ** -0.5),
        'lru_conv_b': nrm(ks[18], (DEPTH, LRU_WIDTH), 0.01),
        'w_rg': nrm(ks[19], (DEPTH, LRU_BLOCKS, LRU_BLOCK_W, LRU_BLOCK_W), LRU_BLOCK_W ** -0.5),
        'b_rg': nrm(ks[20], (DEPTH, LRU_WIDTH), 0.01),
        'w_ig': nrm(ks[21], (DEPTH, LRU_BLOCKS, LRU_BLOCK_W, LRU_BLOCK_W), LRU_BLOCK_W ** -0.5),
        'b_ig': nrm(ks[22], (DEPTH, LRU_WIDTH), 0.01),
        'lru_lambda': jnp.log(a0) - jnp.log1p(-a0),
        'w_out': nrm(ks[23], (DEPTH, D_MODEL, D_MODEL), D_MODEL ** -0.5),
        'g_ffn_norm': gain(ks[24], (DEPTH, D_MODEL)),
        'w_up': nrm(ks[25], (DEPTH, D_MODEL, 2 * D_FF), D_MODEL ** -0.5),
        'ffn_conv_w': nrm(ks[26], (DEPTH, FFN_CONV_W, 2 * D_FF), FFN_CONV_W ** -0.5),
        'ffn_conv_b': nrm(ks[27], (DEPTH, 2 * D_FF), 0.01),
        'w_down': nrm(ks[28], (DEPTH, D_FF, D_MODEL), D_FF ** -0.5),
    }

def reference(x_prompt, x_sample, cache_kv_latent, cache_k_rope, state_lru_h, state_lru_conv,
              state_ffn_conv, g_mix_norm, w_in, g_q_a, w_q_b, g_kv_a, w_kv_b, g_qn, g_qr, g_kn, g_kr,
              lru_conv_w, lru_conv_b, w_rg, b_rg, w_ig, b_ig, lru_lambda, w_out, g_ffn_norm,
              w_up, ffn_conv_w, ffn_conv_b, w_down):
    bp, tp = x_prompt.shape[0], x_prompt.shape[1]
    ts = x_sample.shape[1]
    past = cache_kv_latent.shape[2]
    dt = x_prompt.dtype
    pos_p = jnp.arange(tp, dtype=jnp.int32)
    pos_s = past + jnp.arange(ts, dtype=jnp.int32)
    yp, ys = x_prompt, x_sample
    p_states = [[], [], [], [], []]
    s_states = [[], [], [], [], []]
    for l in range(DEPTH):
        lp = (g_mix_norm[l], w_in[l], g_q_a[l], w_q_b[l], g_kv_a[l], w_kv_b[l], g_qn[l], g_qr[l],
              g_kn[l], g_kr[l], lru_conv_w[l], lru_conv_b[l], w_rg[l], b_rg[l], w_ig[l], b_ig[l],
              lru_lambda[l], w_out[l], g_ffn_norm[l], w_up[l], ffn_conv_w[l], ffn_conv_b[l], w_down[l])
        yp, st_p = hybrid_layer(yp, pos_p,
                                jnp.zeros((bp, 0, KV_LORA), dt), jnp.zeros((bp, 0, ROPE_DIM), dt),
                                jnp.zeros((bp, LRU_WIDTH), dt),
                                jnp.zeros((bp, LRU_CONV_W - 1, LRU_WIDTH), dt),
                                jnp.zeros((bp, FFN_CONV_W - 1, 2 * D_FF), dt), *lp)
        ys, st_s = hybrid_layer(ys, pos_s, cache_kv_latent[l], cache_k_rope[l], state_lru_h[l],
                                state_lru_conv[l], state_ffn_conv[l], *lp)
        for j in range(5):
            p_states[j].append(st_p[j])
            s_states[j].append(st_s[j])
    p_lat, p_kr, p_h, p_conv, p_ffn = [jnp.stack(s, axis=0) for s in p_states]
    s_lat, s_kr, s_h, s_conv, s_ffn = [jnp.stack(s, axis=0) for s in s_states]
    return (yp, ys, p_lat, p_kr, p_h, p_conv, p_ffn, s_lat, s_kr, s_h, s_conv, s_ffn)


_drawn_inputs = setup_inputs


def setup_inputs(seed=0):
    import zlib

    import numpy as np

    out = dict(_drawn_inputs(seed))
    spreads = {}
    factors = {'cache_k_rope': 2.729,
     'g_mix_norm': 5.092,
     'g_q_a': 8.0,
     'g_kv_a': 5.12,
     'g_qn': 8.0,
     'g_qr': 8.0,
     'g_kn': 8.0,
     'g_kr': 4.887,
     'b_rg': 36.64,
     'b_ig': 29.033,
     'g_ffn_norm': 23.057,
     'ffn_conv_b': 23.206,
     'lru_conv_b': 8.0}
    for name, (base, spread) in spreads.items():
        noise = np.random.default_rng([zlib.crc32(name.encode()), seed]).standard_normal(out[name].shape)
        drawn = base * np.exp(spread * noise) if base else spread * noise
        out[name] = __import__('jax').numpy.asarray(drawn.astype(out[name].dtype))
    for name, factor in factors.items():
        out[name] = (out[name] * factor).astype(out[name].dtype)
    return out
```

```python
import numpy as np
import concourse.bass as bass
from concourse import mybir
from concourse.alu_op_type import AluOpType as ALU

F32 = mybir.dt.float32
F32R = mybir.dt.float32r
ACT = mybir.ActivationFunctionType
X = mybir.AxisListType.X
P = 128

D = 1024
KD = D // P
SEQ, DEC, PAST = 512, 32, 512
CHUNK = 64
NH, NOPE, ROPE, VD = 16, 64, 32, 64
QK = NOPE + ROPE
HR = ROPE // 2
QL, KVL = 256, 128
NQ = QL // P
FF = 2816
KF = FF // P
LAT = QL + KVL + ROPE
EPS = 1e-6
THETA = 10000.0
MASKED = -1e30
SCALE = QK ** -0.5

PAD = 4
S0 = SEQ + PAD
T = S0 + DEC
HT = T // 2
LEAD = 4
NK = SEQ + PAST + DEC
NKT = NK // P + 1
LASTP = P - DEC
NT = SEQ // P
TOK = [(i * P, 0, P) for i in range(NT)] + [(S0, LASTP, DEC)]
NTT = len(TOK)

V_GMIX, V_CW, V_CB, V_BR, V_BI, V_LAM, V_H0, V_CS, V_GFF, V_GQA = 0, 8, 40, 48, 56, 64, 72, 80, 104, 112
V_N = V_GQA + NQ
F_W, F_B, F_S = V_N, V_N + 3 * 44, V_N + 4 * 44
NU = 2 * KF
V_ALL = V_N + 6 * NU

I_LAT, I_IN, I_OUT = 0, 4, 28
I_UP = I_OUT + KD
I_DOWN = I_UP + NU
N_ITEMS = I_DOWN + 3 * KD
G_U, G_GA, G_GB, G_OUT, G_UP = 0, 8, 16, 24, 32
G_DOWN = G_UP + NU
DONE = I_IN + 1
NP_ = NH // 2


class Count:

    def __init__(self, sem):
        self.sem, self.n, self.term = sem, 0, 0

    def on(self, instruction, by=1):
        instruction.then_inc(self.sem, by)
        self.n += by
        return self.value()

    def value(self):
        return self.n + self.term if not isinstance(self.term, int) else self.n


class Loop:

    def __init__(self, eng, trips, counts):
        self.fori, self.trips, self.counts = eng.Fori(0, trips), trips, counts

    def __enter__(self):
        i = self.fori.__enter__()
        for c, per in self.counts:
            c.term, c.start = i * per, c.n
        return i

    def __exit__(self, *a):
        for c, per in self.counts:
            assert c.n - c.start == per, (c.sem, c.n - c.start, per)
            c.n += per * (self.trips - 1)
            c.term = 0
        return self.fori.__exit__(*a)


def layer(nc, i, c, o):
    from contextlib import ExitStack
    ctx = ExitStack()
    with ctx:
        base = 16512
        names = [0]

        def at(name, shape, offset, dtype=F32):
            return nc.alloc_sbuf_tensor_at(name, shape, dtype, offset=base + offset)

        XB = KD * T * 4
        place = 0

        def fixed(name, shape, dtype=F32):
            nonlocal place
            n = int(np.prod(shape[1:])) * 4
            t = at(name, shape, place, dtype)
            place += -(-n // 32) * 32
            return t

        ident = fixed("ident", [P, P])
        ones = fixed("ones", [P, P])
        rope = fixed("rope", [P, NTT, 2 * HR])
        bc = fixed("bc", [P, KVL + QK + ROPE])
        gkn = fixed("gkn", [P, 1])
        vec = fixed("vec", [P, V_ALL])
        la_s = fixed("la_s", [P, KD])
        small = fixed("small", [P, 8, 40])
        xT = fixed("xT", [P, KD, T])
        raw = fixed("w_raw", [P, 4, KD * P])
        hi = fixed("w_hi", [P, 2, KD * P], F32R)
        lo = fixed("w_lo", [P, 2, KD * P], F32R)
        region = place
        U = fixed("U", [P, KD, LEAD + T])
        sigA = fixed("sigA", [P, KD, T])
        cqT = fixed("cqT", [P, NQ, T])
        latT = fixed("latT", [P, NK])
        KT = fixed("KT", [P, 4, NK])
        QT = fixed("QT", [P, 4, T])
        xs = place
        xnh = fixed("xnh", [P, KD, T], F32R)
        xnl = fixed("xnl", [P, KD, T], F32R)
        th_at = place
        th = fixed("th", [P, KD, T])
        qs_at = place
        uc = fixed("uc", [P, KD, T])
        tmp_at = place
        tmp = fixed("tmp", [P, 4, T])
        lruw = fixed("lruw", [P, 4, 2, P])
        tmp_end = place
        xnat = at("xnat", [P, NTT, D], th_at)
        xsq = at("xsq", [P, 2, KD, P], region)
        vrows = at("vrows", [P, 4, P], region + 2 * KD * P * 4)
        nat = at("nat", [P, NTT, LAT], region + KD * (LEAD + T) * 4)
        past = at("past", [P, PAST // P, KVL + ROPE], region + KD * (LEAD + T) * 4 + NTT * LAT * 4)
        nsq = at("nsq", [P, NTT, LAT], th_at)
        place = th_at
        mxh = at("mxh", [P, KD, T], xs, F32R)
        mxl = at("mxl", [P, KD, T], xs + XB, F32R)
        V = fixed("V", [P, 2, NKT, 2, VD])
        Kn = fixed("Kn", [P, NKT, 2, NOPE])
        Qn = fixed("Qn", [P, NTT, 2, QK])
        kqs = fixed("kqs", [P, NKT * 2 * NOPE])
        rot = fixed("rot", [P, 4, NTT * 2, HR])
        Pn = fixed("Pn", [P, 2, SEQ])
        Ps = fixed("Ps", [P, PAST + DEC])
        PT = fixed("PT", [P, 2, SEQ])
        PTs = fixed("PTs", [P, 5, 2 * DEC])
        wkv = fixed("wkv", [P, 2, 2 * (NOPE + VD)])
        wq = fixed("wq", [P, 2, NQ, 2 * QK])
        ot = fixed("ot", [P, 2, T])
        att_end = place
        place = region
        x2h = fixed("x2h", [P, KD, T], F32R)
        x2l = fixed("x2l", [P, KD, T], F32R)
        hh = fixed("hh", [P, KF, T], F32R)
        hl = fixed("hl", [P, KF, T], F32R)
        upx = fixed("upx", [P, 4, LEAD + T])
        uct = fixed("uct", [P, 4, T])
        ffn_end = place
        sq2 = at("sq2", [P, 2, T], th_at)
        nrm = at("nrm", [P, 3, T], th_at + 2 * T * 4)
        x2ss = at("x2ss", [P, T], th_at + 6 * T * 4)
        assert th_at + 7 * T * 4 <= ffn_end - 8 * T * 4 - 4 * LEAD * 4
        place = max(tmp_end, att_end, ffn_end)
        st = fixed("st", [P, 8, KD])
        st2 = fixed("st2", [P, 4, NU])
        stT = fixed("stT", [P, P])
        st2T = fixed("st2T", [P, 2, P])
        ynat = at("ynat", [P, 2, 5, P], region)
        yT = at("yT", [P, 2, T], region + 2 * 5 * P * 4)
        assert base + place <= 229368, base + place

        PS = ctx.enter_context(nc.psum_tensor("PS", [P, 8, 512], F32))

        def pair(g):
            return PS[:, 2 * (g % 2):2 * (g % 2) + 2, 0:HT]

        def halves(ap):
            return ap.rearrange("p (a b) -> p a b", a=2)

        def sem(name):
            return ctx.enter_context(nc.semaphore(name))

        s_ident, s_const, s_rows, s_state = sem("ident_in"), sem("const_in"), sem("rows_in"), sem("past_in")
        s_xt = [sem(f"x{t}_in") for t in range(NTT)]
        s_w = [sem(f"w{s}_in") for s in range(4)]
        s_lw = [sem(f"lruw{s}_in") for s in range(4)]
        s_pw = [sem(f"pair_w{s}_in") for s in range(2)]
        s_out, s_lout = sem("stored"), sem("latents_stored")
        s_yout = [sem(f"y{s}_stored") for s in range(2)]

        s_hi, s_lo, s_used = sem("w_hi_done"), sem("w_lo_done"), sem("w_item_multiplied")
        s_free = sem("product_evacuated")
        s_dve, s_act, s_pool = sem("dve_step"), sem("act_step"), sem("pool_step")
        s_vecT, s_vec = sem("vectors_transposed"), sem("vectors_ready")
        s_xTd, s_xTa, s_xTv = sem("x_transposed"), sem("xT_left_half"), sem("xT_right_half")
        s_sq, s_ss, s_ms, s_rsg = sem("squares"), sem("sums_of_squares"), sem("mean_squares"), sem("rsqrt_guess")
        s_xnf, s_xh, s_xl = sem("xn_full"), sem("xn_hi"), sem("xn_lo")
        s_nat = sem("latent_evacuated")
        s_nms, s_nrs, s_nn, s_krr = sem("latent_mean"), sem("latent_rsqrt"), sem("latent_normed"), sem("key_rotated")
        s_lt, s_lte, s_rope4 = sem("latent_transposed"), sem("latent_columns"), sem("key_rope_copied")
        s_uc, s_spe, s_sp = sem("conv_ready"), sem("exp_minus_lambda"), sem("softplus_ready")
        s_lru, s_lrui, s_iu = sem("lru_gates"), sem("lru_gates_read"), sem("lru_gated_input")
        s_a, s_a2, s_m2, s_mult, s_bt = sem("lru_a"), sem("lru_a2"), sem("lru_m2"), sem("lru_mult"), sem("lru_b")
        s_gb, s_rec = sem("sigmoid_b"), sem("gated_recurrence")
        s_stT, s_stc = sem("states_transposed"), sem("states_copied")
        s_clear = sem("cleared")
        s_pj, s_pjf = sem("qkv_product"), sem("qkv_evacuated")
        s_kqs, s_kqm, s_kqr = sem("kq_squares"), sem("kq_mean"), sem("kq_rsqrt")
        s_kn, s_qn, s_qr = sem("k_normed"), sem("q_normed"), sem("q_rotated")
        s_tr, s_trf = sem("kq_transposed"), sem("kq_columns")
        s_s, s_mx, s_e, s_pn = sem("scores"), sem("score_max"), sem("exps"), sem("probs")
        s_pt, s_ptfa, s_ptfv = sem("probs_transposed"), sem("probs_columns_act"), sem("probs_columns_dve")
        s_pv, s_o, s_mx2, s_mh, s_ml = sem("values"), sem("attn_evacuated"), sem("mixed"), sem("mixed_hi"), sem("mixed_lo")
        s_x2q, s_ss2, s_x2t = sem("x2_squares"), sem("x2_squares_added"), sem("x2_sums")
        s_x2z = sem("x2_sums_cleared")
        s_gc, s_sg, s_h2, s_hh, s_hl = sem("gate_conv"), sem("gate_silu"), sem("hidden"), sem("hidden_hi"), sem("hidden_lo")
        s_yt, s_yn = sem("y_transposed"), sem("y_natural")

        block = ctx.enter_context(nc.Block())

        w_in_k = i["w_in"][0].rearrange("(k p) n -> p k n", p=P)
        w_out_k = i["w_out"][0].rearrange("(k p) n -> p k n", p=P)
        w_up_k = i["w_up"][0].rearrange("(k p) n -> p k n", p=P)
        w_down_k = i["w_down"][0].rearrange("(k p) n -> p k n", p=P)
        w_q_k = i["w_q_b"][0].rearrange("(k p) n -> p k n", p=P)
        raw3 = raw[:, :, :].rearrange("p s (k n) -> p s k n", k=KD)

        def one(t, n, *rest):
            return t[(slice(None), bass.ds(n, 1)) + rest] if not isinstance(n, int) else t[(slice(None), slice(n, n + 1)) + rest]

        @block.sync
        def _(sp):
            sp.dma_start(ident[:, :], c["ident"]).then_inc(s_ident, 16)
            for t, (c0, p0, n) in enumerate(TOK):
                src = i["x_prompt"][0, c0:c0 + n, :] if t < NT else i["x_sample"][0]
                sp.dma_start(xnat[0:n, t, :], src).then_inc(s_xt[t], 16)
            for t in range(4):
                sp.dma_start(raw[:, t, 0:2 * LAT].rearrange("p (k n) -> p k n", k=2),
                             w_in_k[:, 2 * t:2 * t + 2, 0:LAT]).then_inc(s_w[t], 16)
            with sp.Fori(0, 6) as it:
                for r in range(4):
                    sp.wait_ge(s_lo, it * 4 + (I_IN + r - 3))
                    sp.dma_start(raw3[:, r], w_in_k[:, :, bass.ds(it * (4 * P) + (LAT + r * P), P)]).then_inc(s_w[r], 16)
            def w_out_items(q):
                for r in range(4):
                    sp.wait_ge(s_lo, q * 4 + (I_OUT + r - 3))
                    sp.dma_start(raw3[:, r], w_out_k[:, :, (4 * q + r) * P:(4 * q + r + 1) * P]).then_inc(s_w[r], 16)

            def pair_weights(p, par):
                sp.dma_start(wkv[:, par, :], i["w_kv_b"][0][:, bass.ds(p * (4 * P) + par * 2 * P, 2 * P)]).then_inc(s_pw[par], 16)
                sp.dma_start(wq[:, par, :, :], w_q_k[:, :, bass.ds(p * (4 * QK) + par * 2 * QK, 2 * QK)]).then_inc(s_pw[par], 16)

            w_out_items(0)
            sp.wait_ge(s_clear, 1)
            pair_weights(0, 0)
            pair_weights(0, 1)
            with sp.Fori(1, NP_ // 2) as it:
                for par in range(2):
                    sp.wait_ge(s_pj, it * 16 + (8 * par - 8))
                    pair_weights(it, par)
            w_out_items(1)
            with sp.Fori(0, NU // 4) as it:
                for r in range(4):
                    sp.wait_ge(s_lo, it * 4 + (I_UP + r - 3))
                    sp.dma_start(raw3[:, r], w_up_k[:, :, bass.ds(it * (2 * P) + ((r // 2) * P + (r % 2) * FF), P)]).then_inc(s_w[r], 16)
            with sp.Fori(0, 2) as it:
                for r in range(12):
                    m, k0 = r // 3, KD * (r % 3)
                    nk = min(KD, KF - k0)
                    sp.wait_ge(s_lo, it * 12 + (I_DOWN + r - 3))
                    sp.dma_start(raw3[:, r % 4, 0:nk], w_down_k[:, k0:k0 + nk, bass.ds(it * (4 * P) + m * P, P)]).then_inc(s_w[r % 4], 16)

        @block.gpsimd
        def _(pool):
            step = Count(s_pool)
            for v0, name, n in ((V_GMIX, "g_mix_norm", 8), (V_CB, "lru_conv_b", 8), (V_BR, "b_rg", 8), (V_BI, "b_ig", 8),
                                (V_LAM, "lru_lambda", 8), (V_H0, "state_lru_h", 8), (V_GFF, "g_ffn_norm", 8), (V_GQA, "g_q_a", NQ)):
                src = i[name][0] if name == "state_lru_h" else i[name]
                pool.dma_start(vrows[v0:v0 + n, 0, :], src.rearrange("a (m p) -> (a m) p", p=P)).then_inc(s_rows, 16)
            pool.dma_start(vrows[V_CW:V_CW + 32, 0, :], i["lru_conv_w"][0].rearrange("j (m p) -> (j m) p", p=P)).then_inc(s_rows, 16)
            pool.dma_start(vrows[V_CS:V_CS + 24, 0, :], i["state_lru_conv"][0, 0].rearrange("j (m p) -> (j m) p", p=P)).then_inc(s_rows, 16)
            fw = i["ffn_conv_w"][0].rearrange("j (m p) -> (j m) p", p=P)
            pool.dma_start(vrows[0:2 * NU, 1, :], fw[0:2 * NU, :]).then_inc(s_rows, 16)
            pool.dma_start(vrows[0:NU, 2, :], fw[2 * NU:3 * NU, :]).then_inc(s_rows, 16)
            pool.dma_start(vrows[NU:2 * NU, 2, :], i["ffn_conv_b"].rearrange("a (m p) -> (a m) p", p=P)).then_inc(s_rows, 16)
            pool.dma_start(vrows[0:2 * NU, 3, :], i["state_ffn_conv"][0, 0].rearrange("j (m p) -> (j m) p", p=P)).then_inc(s_rows, 16)
            pool.dma_start(bc[:, 0:KVL], i["g_kv_a"].broadcast_to([P, KVL])).then_inc(s_const, 16)
            pool.dma_start(bc[:, KVL:KVL + NOPE], i["g_qn"].broadcast_to([P, NOPE])).then_inc(s_const, 16)
            pool.dma_start(bc[:, KVL + NOPE:KVL + QK], i["g_qr"].broadcast_to([P, ROPE])).then_inc(s_const, 16)
            pool.dma_start(bc[:, KVL + QK:], i["g_kr"].broadcast_to([P, ROPE])).then_inc(s_const, 16)
            for h in range(2):
                pool.dma_start(gkn[h * NOPE:(h + 1) * NOPE, :], i["g_kn"].rearrange("a p -> p a")).then_inc(s_const, 16)
            pool.dma_start(rope[:, :, :], c["rope"].rearrange("p (t n) -> p t n", t=NTT)).then_inc(s_const, 16)
            for s in range(4):
                pool.dma_start(KT[QK:QK + NT, s, :], c["kmask"]).then_inc(s_const, 16)
                pool.dma_start(QT[QK:QK + NT, s, :], c["qmask"]).then_inc(s_const, 16)
            pool.dma_start(past[:, :, 0:KVL], i["cache_kv_latent"][0, 0].rearrange("(t p) n -> p t n", p=P)).then_inc(s_state, 16)
            pool.dma_start(past[:, :, KVL:], i["cache_k_rope"][0, 0].rearrange("(t p) n -> p t n", p=P)).then_inc(s_state, 16)

            cos, sin = rope[:, :, 0:HR], rope[:, :, HR:]
            pool.wait_ge(s_const, 16 * 15)
            pool.wait_ge(s_nn, 1)
            k1, k2 = nat[:, :, LAT - ROPE:LAT - HR], nat[:, :, LAT - HR:LAT]
            part = [nsq[:, :, HR * n:HR * (n + 1)] for n in range(4)]
            for dst, a, b in zip(part, (k1, k2, k1, k2), (cos, sin, sin, cos)):
                step.on(nc.gpsimd.tensor_tensor(dst, a, b, ALU.mult))
            pool.wait_ge(s_pool, step.value())
            nc.gpsimd.tensor_tensor(k1, part[0], part[1], ALU.subtract).then_inc(s_krr, 1)
            nc.gpsimd.tensor_tensor(k2, part[2], part[3], ALU.add).then_inc(s_krr, 1)
            pool.wait_ge(s_krr, 2)
            for c0, n, dst_p, dst_s in ((QL, KVL, o[2], o[7]), (QL + KVL, ROPE, o[3], o[8])):
                pool.dma_start(dst_p[0, 0].rearrange("(t p) n -> p t n", p=P), nat[:, 0:NT, c0:c0 + n]).then_inc(s_lout, 16)
                pool.dma_start(dst_s[0, 0], nat[LASTP:P, NT, c0:c0 + n]).then_inc(s_lout, 16)

            def lru_weights(n):
                pool.dma_start(lruw[:, n % 4, 0, :], i["w_rg"][0, n]).then_inc(s_lw[n % 4], 16)
                pool.dma_start(lruw[:, n % 4, 1, :], i["w_ig"][0, n]).then_inc(s_lw[n % 4], 16)

            for n in range(4):
                lru_weights(n)
            pool.wait_ge(s_lte, NTT + 2)
            for s in range(1, 4):
                nc.gpsimd.tensor_copy(KT[NOPE:QK, s, :], KT[NOPE:QK, 0, :]).then_inc(s_rope4, 1)
            pool.wait_ge(s_rope4, 3)
            for n in range(KD):
                pool.wait_ge(s_lrui, n + 1)
                if n < 4:
                    lru_weights(n + 4)
                nc.gpsimd.tensor_tensor(uc[:, n, :], tmp[:, 2 + n % 2, :], uc[:, n, :], ALU.mult).then_inc(s_iu, 1)
            for n in range(KD):
                pool.wait_ge(s_a, n + 1)
                if n >= 2:
                    pool.wait_ge(s_m2, n - 1)
                nc.gpsimd.tensor_tensor(tmp[:, n % 2, :], U[:, n, LEAD:], U[:, n, LEAD:], ALU.mult).then_inc(s_a2, 1)
            pool.wait_ge(s_iu, KD)
            for n in range(KD):
                pool.wait_ge(s_mult, n + 1)
                nc.gpsimd.tensor_tensor(uc[:, n, :], th[:, n, :], uc[:, n, :], ALU.mult).then_inc(s_bt, 1)

            kn3 = Kn[:, :, :, :].rearrange("p t h n -> p (t h) n")
            qn3 = Qn[:, :, :, :].rearrange("p t h n -> p (t h) n")
            q1, q2 = Qn[:, :, :, NOPE:NOPE + HR], Qn[:, :, :, NOPE + HR:]
            ro = rot[:, :, :, :].rearrange("p f (t h) n -> p f t h n", h=2)

            def squares(q):
                pool.wait_ge(s_pjf, q * 8 + 5)
                pool.wait_ge(s_kqm, q * 2)
                nc.gpsimd.tensor_tensor(kqs[:, :].rearrange("p (t n) -> p t n", n=NOPE), kn3, kn3, ALU.mult).then_inc(s_kqs, 1)
                pool.wait_ge(s_pjf, q * 8 + 8)
                pool.wait_ge(s_kqm, q * 2 + 1)
                nc.gpsimd.tensor_tensor(kqs[:, 0:NTT * 2 * QK].rearrange("p (t n) -> p t n", n=QK), qn3, qn3, ALU.mult).then_inc(s_kqs, 1)

            def rotate(q):
                pool.wait_ge(s_qn, q + 1)
                for h in range(2):
                    for n, (a, b) in enumerate(((q1, cos), (q2, sin), (q1, sin), (q2, cos))):
                        step.on(nc.gpsimd.tensor_tensor(ro[:, n, :, h], a[:, :, h], b, ALU.mult))
                pool.wait_ge(s_pool, step.value())
                for h in range(2):
                    nc.gpsimd.tensor_tensor(q1[:, :, h], ro[:, 0, :, h], ro[:, 1, :, h], ALU.subtract)
                    last = nc.gpsimd.tensor_tensor(q2[:, :, h], ro[:, 2, :, h], ro[:, 3, :, h], ALU.add)
                last.then_inc(s_qr, 1)

            pool.wait_ge(s_rec, KD)
            for s in range(2):
                pool.wait_ge(s_pool, step.on(nc.gpsimd.memset(V[0:LASTP, s, NKT - 1, :, :], 0.0)))
            nc.gpsimd.memset(Ps[:, :], 0.0)
            nc.gpsimd.memset(ot[:, :, SEQ:S0], 0.0).then_inc(s_clear, 1)
            squares(0)
            rotate(0)
            with Loop(pool, 3, [(step, 16)]) as it:
                for par in range(2):
                    squares(it * 2 + (par + 1))
                    rotate(it * 2 + (par + 1))
            squares(NP_ - 1)
            rotate(NP_ - 1)
            pool.wait_ge(s_ml, KD)
            nc.gpsimd.memset(x2ss[:, :], 0.0).then_inc(s_x2z, 1)
            pool.wait_ge(s_x2z, 1)
            with pool.Fori(0, 2) as it:
                for r in range(4):
                    pool.wait_ge(s_x2q, it * 4 + (r + 1))
                    pool.wait_ge(s_ss2, it * 4 + r)
                    nc.gpsimd.tensor_tensor(x2ss[:, :], x2ss[:, :], sq2[:, r % 2, :], ALU.add).then_inc(s_ss2, 1)
            pool.wait_ge(s_lout, 64)
            pool.wait_ge(s_stc, 1)
            pool.dma_start(o[4][0].rearrange("a (m p) -> (a m) p", p=P), stT[0:8, :]).then_inc(s_out, 16)
            pool.dma_start(o[9][0].rearrange("a (m p) -> (a m) p", p=P), stT[8:16, :]).then_inc(s_out, 16)
            pool.dma_start(o[5][0, 0].rearrange("j (m p) -> (j m) p", p=P), stT[16:40, :]).then_inc(s_out, 16)
            pool.dma_start(o[10][0, 0].rearrange("j (m p) -> (j m) p", p=P), stT[40:64, :]).then_inc(s_out, 16)
            pool.wait_ge(s_stc, 2)
            pool.dma_start(o[6][0, 0].rearrange("j (m p) -> (j m) p", p=P), st2T[0:2 * NU, 0, :]).then_inc(s_out, 16)
            pool.dma_start(o[11][0, 0].rearrange("j (m p) -> (j m) p", p=P), st2T[0:2 * NU, 1, :]).then_inc(s_out, 16)
            y_p = o[0][0].rearrange("(t p) n -> p t n", p=P)
            for m in range(KD):
                pool.wait_ge(s_yn, 2 * m + 2)
                pool.dma_start(y_p[:, :, m * P:(m + 1) * P], ynat[:, m % 2, 0:NT, :]).then_inc(s_yout[m % 2], 16)
                pool.dma_start(o[1][0][:, m * P:(m + 1) * P], ynat[0:DEC, m % 2, NT, :]).then_inc(s_yout[m % 2], 16)
            pool.wait_ge(s_out, 16 * 6)
            for s in range(2):
                pool.wait_ge(s_yout[s], 16 * KD)

        @block.scalar
        def _(act):
            step = Count(s_act)

            def link(ins):
                act.wait_ge(s_act, step.on(ins))

            def split_hi(t, slot, loaded, n=KD * P):
                act.wait_ge(s_w[slot % 4], loaded)
                if not isinstance(t, int) or t >= 2:
                    act.wait_ge(s_used, t - 1)
                nc.scalar.activation(hi[:, slot % 2, 0:n], raw[:, slot % 4, 0:n], ACT.Copy).then_inc(s_hi, 1)

            def rsqrt_guess(dst, src, sem_):
                link(nc.scalar.activation(dst, src, ACT.Ln))
                nc.scalar.activation(dst, dst, ACT.Exp, scale=-0.5).then_inc(sem_, 1)

            def xT_left(t):
                c0, _, n = TOK[t]
                act.wait_ge(s_xTd, t + 1)
                nc.scalar.activation(xT[:, 0:4, c0:c0 + n], PS[:, 2 * (t % 2), :].rearrange("p (k n) -> p k n", k=4)[:, :, 0:n],
                                     ACT.Copy).then_inc(s_xTa, 1)

            def x_squares(t):
                c0, _, n = TOK[t]
                act.wait_ge(s_xTa, t + 1)
                act.wait_ge(s_xTv, t + 1)
                if t >= 2:
                    act.wait_ge(s_ss, t - 1)
                nc.scalar.activation(xsq[:, t % 2, :, 0:n], xT[:, :, c0:c0 + n], ACT.Square).then_inc(s_sq, 1)

            for t in range(NTT):
                xT_left(t)
                x_squares(t)
            act.wait_ge(s_vecT, 1)
            nc.scalar.activation(vec[:, 0:V_ALL], PS[:, 6, 0:V_ALL], ACT.Copy).then_inc(s_vec, 1)
            act.wait_ge(s_vec, 1)
            nc.scalar.activation(la_s[:, :], vec[:, V_LAM:V_LAM + KD], ACT.Exp, scale=-1.0).then_inc(s_spe, 1)
            act.wait_ge(s_ms, 1)
            rsqrt_guess(tmp[:, 1, :], tmp[:, 0, :], s_rsg)
            for t in range(2):
                split_hi(t, t, 16, 2 * LAT)
            for k in range(KD):
                act.wait_ge(s_xnf, k + 1)
                nc.scalar.activation(xnh[:, k, :], tmp[:, 2 + k % 2, :], ACT.Copy).then_inc(s_xh, 1)
            for t in range(2, 4):
                split_hi(t, t, 16, 2 * LAT)
            for t in range(4, 6):
                split_hi(t, t, 32)
            act.wait_ge(s_used, I_IN)
            for t in range(NTT):
                nc.scalar.activation(nat[:, t, :], PS[:, 3 + t, 0:LAT], ACT.Copy).then_inc(s_nat, 1)
            act.wait_ge(s_nms, 1)
            rsqrt_guess(small[:, 1, 0:3 * NTT], small[:, 0, 0:3 * NTT], s_nrs)

            with act.Fori(0, 2) as it:
                for r in range(4):
                    act.wait_ge(s_used, it * 4 + (G_U + r + DONE))
                    nc.scalar.activation(halves(one(U, it * 4 + r, slice(LEAD, None))[:, 0]), pair(r), ACT.Copy).then_inc(s_free, 1)
                    split_hi(it * 4 + (I_IN + r + 2), r + 2, it * 16 + 16 * (2 + (r + 2) // 4))
            act.wait_ge(s_lt, NTT + 2)
            act.wait_ge(s_lte, NTT + 2)
            act.wait_ge(s_lout, 64)
            act.wait_ge(s_uc, KD)
            with act.Fori(0, 2) as it:
                for r in range(4):
                    n = it * 4 + r
                    act.wait_ge(s_used, it * 4 + (G_GA + r + DONE))
                    nc.scalar.activation(halves(one(sigA, n, slice(None))[:, 0]), pair(r), ACT.Sigmoid).then_inc(s_free, 1)
                    split_hi(it * 4 + (I_IN + 8 + r + 2), r + 2, it * 16 + 16 * (4 + (r + 2) // 4))
                    act.wait_ge(s_lru, n + 1)
                    u_n = one(U, n, slice(LEAD, None))[:, 0]
                    nc.scalar.activation(halves(u_n), PS[:, 4:6, 0:HT], ACT.Sigmoid, bias=vec[:, bass.ds(it * 4 + (V_BR + r), 1)]).then_inc(s_act, 1)
                    act.wait_ge(s_iu, it * 4 + (r - 1) if r else it * 3)
                    nc.scalar.activation(halves(tmp[:, 2 + r % 2, :]), PS[:, 6:8, 0:HT], ACT.Sigmoid, bias=vec[:, bass.ds(it * 4 + (V_BI + r), 1)]).then_inc(s_lrui, 1)
                    act.wait_ge(s_act, it * 8 + (step.n + 2 * r + 1))
                    if r == 0:
                        act.wait_ge(s_sp, 1)
                    nc.scalar.activation(one(th, n, slice(None))[:, 0], u_n, ACT.Tanh, scale=la_s[:, bass.ds(n, 1)]).then_inc(s_act, 1)
            step.n += 16
            act.wait_ge(s_act, step.n)
            for n in range(KD):
                nc.scalar.activation(U[:, n, LEAD:], U[:, n, LEAD:], ACT.Exp, scale=la_s[:, n:n + 1]).then_inc(s_a, 1)
            for n in range(KD):
                act.wait_ge(s_m2, n + 1)
                nc.scalar.activation(th[:, n, :], th[:, n, :], ACT.Sqrt, scale=-1.0).then_inc(s_mult, 1)
            with act.Fori(0, 2) as it:
                for r in range(4):
                    act.wait_ge(s_used, it * 4 + (G_GB + r + DONE))
                    act.wait_ge(s_rec, it * 4 + (r - 1) if r else it * 3)
                    nc.scalar.activation(halves(tmp[:, 2 + r % 2, :]), pair(r), ACT.Sigmoid).then_inc(s_free, 1)
                    split_hi(it * 4 + (I_IN + 16 + r + 2), r + 2, it * 16 + 16 * (6 + (r + 2) // 4))

            def evacuate_qkv(q, par, values_before):
                act.wait_ge(s_tr, q * 5)
                for u in range(8):
                    act.wait_ge(s_pj, q * 8 + (u + 1))
                    bank = PS[:, u % 3, :]
                    if u < 5:
                        tiles = 2 if u < 4 else 1
                        kv = bank[:, 0:tiles * 2 * P].rearrange("p (t h n) -> p t h n", t=tiles, h=2)
                        p0 = 0 if u < 4 else LASTP
                        for a in range(tiles):
                            nc.scalar.activation(Kn[:, 2 * u + a, :, :], kv[:, a, :, 0:NOPE], ACT.Copy)
                        if u == 0:
                            act.wait_ge(s_pv, values_before)
                        for a in range(tiles):
                            last = nc.scalar.activation(V[p0:, par, 2 * u + a, :, :], kv[p0:, a, :, NOPE:], ACT.Copy)
                    else:
                        t0 = 2 * (u - 5)
                        tiles = 2 if u < 7 else 1
                        last = nc.scalar.activation(Qn[:, t0:t0 + tiles, :, :].rearrange("p t h n -> p (t h n)"),
                                                    bank[:, 0:tiles * 2 * QK], ACT.Copy)
                    last.then_inc(s_pjf, 1)

            def kq_rsqrt(q):
                act.wait_ge(s_kqm, q * 2 + 2)
                rsqrt_guess(small[:, 1, 0:38], small[:, 0, 0:38], s_kqr)

            def exps(p, n):
                act.wait_ge(s_mx, p * 9 + (n + 1))
                if n < 8:
                    w = (n % 4 + 1) * P
                    act.wait_ge(s_pt, p * 9 + max(n - 1, 0))
                    nc.scalar.activation(Pn[:, n % 2, 0:w], PS[:, 4 + n % 2, 0:w], ACT.Exp, bias=small[:, 4 + n % 2, 2:3],
                                         accum_out=small[:, 4 + n % 2, 0:1]).then_inc(s_e, 1)
                else:
                    act.wait_ge(s_pt, p * 9)
                    R2 = 2 * DEC
                    nc.scalar.activation(Ps[0:R2, 0:PAST], PS[0:R2, 4, :], ACT.Exp, bias=small[0:R2, 6, 2:3],
                                         accum_out=small[0:R2, 6, 5:6])
                    nc.scalar.activation(Ps[0:R2, PAST:], PS[0:R2, 5, 0:DEC], ACT.Exp, bias=small[0:R2, 6, 2:3],
                                         accum_out=small[0:R2, 6, 6:7]).then_inc(s_e, 1)

            def probs_columns(p, n):
                act.wait_ge(s_pt, p * 9 + (n + 1))
                act.wait_ge(s_pv, p * 9 + max(n - 1, 0))
                if n < 8:
                    w = (n % 4 + 1) * P
                    nc.scalar.activation(PT[:, n % 2, 0:w], PS[:, 6, 0:w], ACT.Copy).then_inc(s_ptfa, 1)
                else:
                    nc.scalar.activation(PTs[:, :, :].rearrange("p a b -> p (a b)"), PS[:, 6, 0:5 * 2 * DEC], ACT.Copy).then_inc(s_ptfa, 1)

            def attend(p, par, following):
                if following:
                    evacuate_qkv(p + 1, 1 - par, p * 9)
                exps(p, 0)
                for n in range(9):
                    if n < 8:
                        exps(p, n + 1)
                    if following and n == 2:
                        kq_rsqrt(p + 1)
                    if n % 2 == 0:
                        probs_columns(p, n)
                act.wait_ge(s_mx2, p + 1)
                nc.scalar.activation(one(mxh, p, slice(None))[:, 0], ot[:, par, :], ACT.Copy).then_inc(s_mh, 1)

            act.wait_ge(s_clear, 1)
            act.wait_ge(s_used, I_OUT)
            evacuate_qkv(0, 0, 0)
            kq_rsqrt(0)
            with Loop(act, 3, [(step, 2)]) as it:
                attend(it * 2, 0, True)
                attend(it * 2 + 1, 1, True)
            attend(6, 0, True)
            attend(7, 1, False)

            with act.Fori(0, 2) as it:
                for r in range(4):
                    m = it * 4 + r
                    act.wait_ge(s_free, it * 4 + (G_OUT + r + 1))
                    act.wait_ge(s_ss2, it * 4 + (r - 1) if r else it * 3)
                    nc.scalar.activation(sq2[:, r % 2, :], one(xT, m, slice(None))[:, 0], ACT.Square).then_inc(s_x2q, 1)
                    split_hi(it * 4 + (I_OUT + r + 2), r + 2, it * 16 + 16 * (8 + (r + 2) // 4))
            act.wait_ge(s_stT, 1)
            nc.scalar.activation(stT[0:64, :], PS[0:64, 7, 0:P], ACT.Copy).then_inc(s_stc, 1)
            act.wait_ge(s_ms, 2)
            rsqrt_guess(nrm[:, 1, :], nrm[:, 0, :], s_rsg)
            for k in range(KD):
                act.wait_ge(s_xnf, KD + k + 1)
                nc.scalar.activation(x2h[:, k, :], uct[:, k % 2, :], ACT.Copy).then_inc(s_xh, 1)

            with act.Fori(0, NU // 4) as it:
                for r in range(4):
                    j = r // 2
                    act.wait_ge(s_used, it * 4 + (G_UP + r + DONE))
                    if r == 0:
                        act.wait_ge(s_gc, it * 4)
                    nc.scalar.activation(halves(upx[:, r, LEAD:]), pair(r), ACT.Copy).then_inc(s_free, 1)
                    split_hi(it * 4 + (I_UP + r + 2), r + 2, it * 16 + 16 * (10 + (r + 2) // 4))
                    if r % 2 == 1:
                        act.wait_ge(s_gc, it * 4 + (2 * j + 1))
                        nc.scalar.activation(uct[:, j, :], uct[:, j, :], ACT.Silu,
                                             bias=vec[:, bass.ds(it * 2 + (F_B + j), 1)]).then_inc(s_sg, 1)
                        act.wait_ge(s_h2, it * 2 + (j + 1))
                        nc.scalar.activation(one(hh, it * 2 + j, slice(None))[:, 0], uct[:, 2 + j, :], ACT.Copy).then_inc(s_hh, 1)
            act.wait_ge(s_stT, 2)
            nc.scalar.activation(st2T[0:2 * NU, :, :], PS[0:2 * NU, 7, 0:2 * P].rearrange("p (a b) -> p a b", a=2), ACT.Copy).then_inc(s_stc, 1)

            def y_natural(m, s):
                act.wait_ge(s_yt, m + 1)
                act.wait_ge(s_yout[s], 32 * (m // 2))
                nc.scalar.activation(ynat[:, s, 0:NT, :], PS[:, 4 + 2 * s, :].rearrange("p (a b) -> p a b", a=NT), ACT.Copy).then_inc(s_yn, 1)
                nc.scalar.activation(ynat[0:DEC, s, NT, :], PS[0:DEC, 5 + 2 * s, 0:P], ACT.Copy).then_inc(s_yn, 1)

            for m in range(KD):
                for q in range(3):
                    t = I_DOWN + 3 * m + q + 2
                    if t < N_ITEMS:
                        split_hi(t, t, 16 * (t // 4 + 1), min(KD, KF - KD * ((t - I_DOWN) % 3)) * P)
                if m >= 1:
                    y_natural(m - 1, (m - 1) % 2)
            y_natural(KD - 1, (KD - 1) % 2)

        @block.vector
        def _(dve):
            step = Count(s_dve)
            tt, ts, stt = nc.vector.tensor_tensor, nc.vector.tensor_scalar, nc.vector.scalar_tensor_tensor

            def link(ins):
                dve.wait_ge(s_dve, step.on(ins))

            def split_lo(t, slot, n=KD * P):
                dve.wait_ge(s_hi, t + 1)
                tt(lo[:, slot % 2, 0:n], raw[:, slot % 4, 0:n], hi[:, slot % 2, 0:n].bitcast(F32), ALU.subtract).then_inc(s_lo, 1)

            def newton(y, v, t):
                link(tt(t, y, y, ALU.mult))
                link(tt(t, t, v, ALU.mult))
                link(ts(t, t, -0.5, 1.5, ALU.mult, ALU.add))
                link(tt(y, y, t, ALU.mult))

            nc.vector.memset(xT[:, :, SEQ:S0], 0.0)
            nc.vector.memset(cqT[:, :, SEQ:S0], 0.0)
            nc.vector.memset(tmp[:, 0, :], 1.0)
            nc.vector.memset(ones[:, :], 1.0)

            for t, (c0, _, n) in enumerate(TOK):
                dve.wait_ge(s_xTd, t + 1)
                nc.vector.tensor_copy(xT[:, 4:8, c0:c0 + n], PS[:, 2 * (t % 2) + 1, :].rearrange("p (k n) -> p k n", k=4)[:, :, 0:n]).then_inc(s_xTv, 1)
            dve.wait_ge(s_ss, NTT)
            ts(tmp[:, 0, 0:SEQ], PS[:, 4, :], 1.0 / D, EPS, ALU.mult, ALU.add)
            ts(tmp[:, 0, S0:], PS[:, 5, 0:DEC], 1.0 / D, EPS, ALU.mult, ALU.add).then_inc(s_ms, 1)
            dve.wait_ge(s_spe, 1)
            e, q, q2, acc, mxl_ = (small[:, 2, 8 * n:8 * n + 8] for n in range(5))
            lam = vec[:, V_LAM:V_LAM + KD]
            link(nc.vector.reciprocal(q, la_s[:, :]))
            link(tt(e, la_s[:, :], q, ALU.min))
            link(ts(q, e, 2.0, None, ALU.add))
            link(nc.vector.reciprocal(q2, q))
            link(tt(q, e, q2, ALU.mult))
            link(tt(q2, q, q, ALU.mult))
            link(ts(acc, q2, 1.0 / 19, 1.0 / 17, ALU.mult, ALU.add))
            for d in (15, 13, 11, 9, 7, 5, 3, 1):
                link(tt(acc, acc, q2, ALU.mult))
                link(ts(acc, acc, 1.0 / d, None, ALU.add))
            link(tt(acc, acc, q, ALU.mult))
            link(ts(mxl_, lam, -1.0, 0.0, ALU.mult, ALU.max))
            link(stt(acc, acc, 2.0, mxl_, ALU.mult, ALU.add))
            ts(la_s[:, :], acc, -8.0, None, ALU.mult).then_inc(s_sp, 1)

            dve.wait_ge(s_rsg, 1)
            newton(tmp[:, 1, :], tmp[:, 0, :], tmp[:, 2, :])

            def xn(dst, src, k, g0, rs, count):
                s = k % 2
                if k >= 2:
                    dve.wait_ge(s_xh, count + k - 1)
                    dve.wait_ge(s_xl, count + k - 1)
                stt(dst[:, s, :], src[:, k, :], vec[:, g0 + k:g0 + k + 1], rs, ALU.mult, ALU.mult).then_inc(s_xnf, 1)

            def xn_lo(dst, k, high, low, count):
                dve.wait_ge(s_xh, count + k + 1)
                tt(low[:, k, :], dst[:, k % 2, :], high[:, k, :].bitcast(F32), ALU.subtract).then_inc(s_xl, 1)

            for k in range(KD):
                xn(tmp[:, 2:4, :], xT, k, V_GMIX, tmp[:, 1, :], 0)
                if k == 0:
                    split_lo(0, 0, 2 * LAT)
                else:
                    xn_lo(tmp[:, 2:4, :], k - 1, xnh, xnl, 0)
            xn_lo(tmp[:, 2:4, :], KD - 1, xnh, xnl, 0)
            for t in range(1, 4):
                split_lo(t, t, 2 * LAT)
            for t in range(4, 6):
                split_lo(t, t)

            dve.wait_ge(s_nat, NTT)
            dve.wait_ge(s_const, 16 * 15)
            link(tt(nsq[:, :, :], nat[:, :, :], nat[:, :, :], ALU.mult))
            ms = small[:, 0, 0:3 * NTT].rearrange("p (a t) -> p a t", a=3)
            parts = ((0, QL), (QL, KVL), (QL + KVL, ROPE))
            for a, (c0, n) in enumerate(parts):
                nc.vector.tensor_reduce(ms[:, a, :], nsq[:, :, c0:c0 + n], X, ALU.add).then_inc(s_dve, 1)
                step.n += 1
            dve.wait_ge(s_dve, step.n)
            for a, (c0, n) in enumerate(parts):
                last = ts(ms[:, a, :], ms[:, a, :], 1.0 / n, EPS, ALU.mult, ALU.add)
            last.then_inc(s_nms, 1)
            link(ts(bc[:, KVL:KVL + QK], bc[:, KVL:KVL + QK], SCALE, None, ALU.mult))
            dve.wait_ge(s_nrs, 1)
            newton(small[:, 1, 0:3 * NTT], small[:, 0, 0:3 * NTT], small[:, 2, 0:3 * NTT])
            for t in range(NTT):
                rs = [small[:, 1, a * NTT + t:a * NTT + t + 1] for a in range(3)]
                ts(nat[:, t, 0:QL], nat[:, t, 0:QL], rs[0], None, ALU.mult)
                stt(nat[:, t, QL:QL + KVL], nat[:, t, QL:QL + KVL], rs[1], bc[:, 0:KVL], ALU.mult, ALU.mult)
                last = stt(nat[:, t, QL + KVL:], nat[:, t, QL + KVL:], rs[2], bc[:, KVL + QK:], ALU.mult, ALU.mult)
            last.then_inc(s_nn, 1)

            nc.vector.memset(U[:, :, 0:LEAD], 0.0).then_inc(s_dve, 1)
            step.n += 1
            with Loop(dve, 2, [(step, 20)]) as it:
                for r in range(4):
                    n = it * 4 + r
                    u_n = one(U, n, slice(None))[:, 0]
                    c_n = one(uc, n, slice(None))[:, 0]
                    dve.wait_ge(s_free, it * 4 + (G_U + r + 1))
                    carried = vec[:, V_CS:V_CS + 24].rearrange("p (j m) -> p m j", j=3)
                    link(nc.vector.tensor_copy(u_n[:, LEAD + S0 - 3:LEAD + S0], carried[:, bass.ds(n, 1), :][:, 0]))
                    w = [vec[:, bass.ds(it * 4 + (V_CW + 8 * j + r), 1)] for j in range(4)]
                    b = vec[:, bass.ds(it * 4 + (V_CB + r), 1)]
                    link(ts(c_n, u_n[:, 1:1 + T], w[0], b, ALU.mult, ALU.add))
                    for j in (1, 2):
                        link(stt(c_n, u_n[:, 1 + j:1 + j + T], w[j], c_n, ALU.mult, ALU.add))
                    step.on(stt(c_n, u_n[:, 4:4 + T], w[3], c_n, ALU.mult, ALU.add))
                    split_lo(it * 4 + (I_IN + r + 2), r + 2)
                    tail = u_n[:, LEAD + T - 72:].rearrange("p (a b) -> p a b", b=36)[:, :, 33:36]
                    out_ = st[:, 2:8, :].rearrange("p (a b) m -> p m a b", a=2)
                    nc.vector.tensor_copy(out_[:, bass.ds(n, 1)][:, 0], tail).then_inc(s_uc, 1)

            for t, (c0, _, n) in enumerate(TOK):
                dve.wait_ge(s_lt, t + 1)
                bank = PS[:, 4 + t % 4, :]
                for a in range(NQ):
                    ts(cqT[:, a, c0:c0 + n], bank[:, a * P:a * P + n], vec[:, V_GQA + a:V_GQA + a + 1], None, ALU.mult)
                k0 = c0 if t < NT else SEQ + PAST
                nc.vector.tensor_copy(latT[:, k0:k0 + n], bank[:, 2 * P:2 * P + n])
                nc.vector.tensor_copy(KT[NOPE:QK, 0, k0:k0 + n], bank[NOPE:QK, 3 * P:3 * P + n]).then_inc(s_lte, 1)
            dve.wait_ge(s_lt, NTT + 1)
            nc.vector.tensor_copy(latT[:, SEQ:SEQ + PAST], PS[:, 5, :]).then_inc(s_lte, 1)
            dve.wait_ge(s_lt, NTT + 2)
            nc.vector.tensor_copy(KT[NOPE:QK, 0, SEQ:SEQ + PAST], PS[NOPE:QK, 6, :]).then_inc(s_lte, 1)

            with dve.Fori(0, 2) as it:
                for r in range(4):
                    split_lo(it * 4 + (I_IN + 8 + r + 2), r + 2)
            for n in range(KD):
                dve.wait_ge(s_a2, n + 1)
                stt(th[:, n, :], tmp[:, n % 2, :], 1.0, th[:, n, :], ALU.add, ALU.mult).then_inc(s_m2, 1)
            dve.wait_ge(s_bt, KD)
            nc.vector.memset(U[:, :, LEAD + S0 - 1:LEAD + S0], 0.0)
            link(nc.vector.tensor_copy(uc[:, :, S0 - 1:S0], vec[:, V_H0:V_H0 + KD].unsqueeze(2)))
            with Loop(dve, 2, [(step, 8)]) as it:
                for r in range(4):
                    n = it * 4 + r
                    a_n = one(U, n, slice(LEAD, None))[:, 0]
                    split_lo(it * 4 + (I_IN + 16 + r + 2), r + 2)
                    link(nc.vector.tensor_tensor_scan(a_n, a_n, one(uc, n, slice(None))[:, 0], 0.0, ALU.mult, ALU.add))
                    ends = a_n[:, T - 72:].rearrange("p (a b) -> p a b", b=36)[:, :, 35:36]
                    link(nc.vector.tensor_copy(st[:, 0:2, bass.ds(n, 1)], ends))
                    dve.wait_ge(s_free, it * 4 + (G_GB + r + 1))
                    tt(a_n, a_n, tmp[:, 2 + r % 2, :], ALU.mult).then_inc(s_rec, 1)

            sq3 = kqs[:, :].rearrange("p (t n) -> p t n", n=NOPE)
            sq4 = kqs[:, 0:NTT * 2 * QK].rearrange("p (t n) -> p t n", n=QK)
            kn3 = Kn[:, :, :, :].rearrange("p t h n -> p (t h) n")
            qn3 = Qn[:, :, :, :].rearrange("p t h n -> p (t h) n")

            def key_sums(q):
                dve.wait_ge(s_kqs, q * 2 + 1)
                nc.vector.tensor_reduce(small[:, 0, 0:18], sq3, X, ALU.add).then_inc(s_kqm, 1)

            def query_sums(q):
                dve.wait_ge(s_kqs, q * 2 + 2)
                nc.vector.tensor_reduce(small[:, 0, 18:28], sq4[:, :, 0:NOPE], X, ALU.add)
                link(nc.vector.tensor_reduce(small[:, 0, 28:38], sq4[:, :, NOPE:], X, ALU.add))
                ts(small[:, 0, 0:28], small[:, 0, 0:28], 1.0 / NOPE, EPS, ALU.mult, ALU.add)
                ts(small[:, 0, 28:38], small[:, 0, 28:38], 1.0 / ROPE, EPS, ALU.mult, ALU.add).then_inc(s_kqm, 1)

            def normalise(q):
                dve.wait_ge(s_kqr, q + 1)
                newton(small[:, 1, 0:38], small[:, 0, 0:38], small[:, 2, 0:38])
                y = small[:, 1, :].unsqueeze(2)
                tt(kn3, kn3, y[:, 0:18].to_broadcast([P, 18, NOPE]), ALU.mult).then_inc(s_kn, 1)
                tt(qn3[:, :, 0:NOPE], qn3[:, :, 0:NOPE], y[:, 18:28].to_broadcast([P, 10, NOPE]), ALU.mult)
                link(tt(qn3[:, :, NOPE:], qn3[:, :, NOPE:], y[:, 28:38].to_broadcast([P, 10, ROPE]), ALU.mult))
                gains = bc[:, KVL:KVL + QK].unsqueeze(1).to_broadcast([P, 10, QK])
                tt(qn3, qn3, gains, ALU.mult).then_inc(s_qn, 1)

            def columns(q, par, v):
                bank = PS[:, (8 + v) % 3, :]
                dve.wait_ge(s_tr, q * 5 + (v + 1))
                if v < 3:
                    k0, c0, n = (v * 512, 0, 512) if v < 2 else (SEQ + PAST, LASTP, DEC)
                    for h in range(2):
                        ins = ts(KT[0:NOPE, 2 * par + h, k0:k0 + n], bank[h * NOPE:(h + 1) * NOPE, c0:c0 + n],
                                 gkn[h * NOPE:(h + 1) * NOPE, :], None, ALU.mult)
                        if v == 2:
                            ins = nc.vector.tensor_copy(QT[0:QK, 2 * par + h, S0:], bank[0:QK, P + h * DEC:P + (h + 1) * DEC])
                else:
                    ins = nc.vector.tensor_copy(QT[0:QK, 2 * par + v - 3, 0:SEQ], bank[0:QK, :])
                ins.then_inc(s_trf, 1)

            def row_max(p, n):
                dve.wait_ge(s_s, p * 9 + (n + 1))
                if n < 8:
                    w = (n % 4 + 1) * P
                    nc.vector.tensor_reduce(small[:, 4 + n % 2, 2:3], PS[:, 4 + n % 2, 0:w], X, ALU.max, negate=True).then_inc(s_mx, 1)
                else:
                    R2 = 2 * DEC
                    nc.vector.tensor_reduce(small[0:R2, 6, 3:4], PS[0:R2, 4, :], X, ALU.max, negate=True)
                    link(nc.vector.tensor_reduce(small[0:R2, 6, 4:5], PS[0:R2, 5, 0:DEC], X, ALU.max, negate=True))
                    tt(small[0:R2, 6, 2:3], small[0:R2, 6, 3:4], small[0:R2, 6, 4:5], ALU.min).then_inc(s_mx, 1)

            def normalise_probs(p, n):
                dve.wait_ge(s_e, p * 9 + (n + 1))
                if n < 8:
                    w = (n % 4 + 1) * P
                    link(nc.vector.reciprocal(small[:, 4 + n % 2, 1:2], small[:, 4 + n % 2, 0:1]))
                    ts(Pn[:, n % 2, 0:w], Pn[:, n % 2, 0:w], small[:, 4 + n % 2, 1:2], None, ALU.mult).then_inc(s_pn, 1)
                else:
                    R2 = 2 * DEC
                    link(tt(small[0:R2, 6, 0:1], small[0:R2, 6, 5:6], small[0:R2, 6, 6:7], ALU.add))
                    link(nc.vector.reciprocal(small[0:R2, 6, 1:2], small[0:R2, 6, 0:1]))
                    ts(Ps[0:R2, :], Ps[0:R2, :], small[0:R2, 6, 1:2], None, ALU.mult).then_inc(s_pn, 1)

            def attend(p, par, following):
                row_max(p, 0)
                for n in range(9):
                    if n < 8:
                        row_max(p, n + 1)
                    normalise_probs(p, n)
                    if n % 2 == 1:
                        w = (n % 4 + 1) * P
                        dve.wait_ge(s_pt, p * 9 + (n + 1))
                        dve.wait_ge(s_pv, p * 9 + max(n - 1, 0))
                        nc.vector.tensor_copy(PT[:, 1, 0:w], PS[:, 7, 0:w]).then_inc(s_ptfv, 1)
                    if following:
                        if n == 1:
                            key_sums(p + 1)
                            query_sums(p + 1)
                        if n == 3:
                            normalise(p + 1)
                        if n >= 4:
                            columns(p + 1, 1 - par, n - 4)
                a_p = one(sigA, p, slice(None))[:, 0]
                dve.wait_ge(s_pv, p * 9 + 8)
                tt(ot[:, par, 0:SEQ], PS[:, 3, :], a_p[:, 0:SEQ], ALU.mult).then_inc(s_o, 1)
                dve.wait_ge(s_pv, p * 9 + 9)
                tt(ot[:, par, S0:], PS[:, 3, 0:DEC], a_p[:, S0:], ALU.mult).then_inc(s_o, 1)
                dve.wait_ge(s_o, p * 2 + 2)
                tt(ot[:, par, :], ot[:, par, :], one(U, p, slice(LEAD, None))[:, 0], ALU.add).then_inc(s_mx2, 1)
                dve.wait_ge(s_mh, p + 1)
                tt(one(mxl, p, slice(None))[:, 0], ot[:, par, :], one(mxh, p, slice(None))[:, 0].bitcast(F32), ALU.subtract).then_inc(s_ml, 1)

            dve.wait_ge(s_used, I_OUT)
            key_sums(0)
            query_sums(0)
            normalise(0)
            dve.wait_ge(s_rope4, 3)
            for v in range(5):
                columns(0, 0, v)
            with Loop(dve, 3, [(step, 34)]) as it:
                attend(it * 2, 0, True)
                attend(it * 2 + 1, 1, True)
            attend(6, 0, True)
            attend(7, 1, False)

            with dve.Fori(0, 2) as it:
                for r in range(4):
                    m = it * 4 + r
                    x_m = one(xT, m, slice(None))[:, 0]
                    dve.wait_ge(s_used, it * 4 + (G_OUT + r + DONE))
                    tt(halves(x_m), pair(r), halves(x_m), ALU.add).then_inc(s_free, 1)
                    split_lo(it * 4 + (I_OUT + r + 2), r + 2)
            nc.vector.memset(upx[:, :, 0:LEAD], 0.0)
            dve.wait_ge(s_x2t, 1)
            ts(halves(nrm[:, 0, :]), PS[:, 4:6, 0:HT], 1.0 / D, EPS, ALU.mult, ALU.add).then_inc(s_ms, 1)
            dve.wait_ge(s_rsg, 2)
            newton(nrm[:, 1, :], nrm[:, 0, :], nrm[:, 2, :])
            for k in range(KD):
                xn(uct, xT, k, V_GFF, nrm[:, 1, :], KD)
                if k:
                    xn_lo(uct, k - 1, x2h, x2l, KD)
            xn_lo(uct, KD - 1, x2h, x2l, KD)

            with Loop(dve, NU // 4, [(step, 16)]) as it:
                for r in range(4):
                    j, is_value = divmod(r, 2)
                    u_r = upx[:, r, :]
                    dst = uct[:, 2 * is_value + j, :]
                    m0 = j + KF * is_value
                    split_lo(it * 4 + (I_UP + r + 2), r + 2)
                    dve.wait_ge(s_free, it * 4 + (G_UP + r + 1))
                    carried = vec[:, F_S:F_S + 2 * NU].rearrange("p (s m) -> p m s", s=2)
                    link(nc.vector.tensor_copy(u_r[:, LEAD + S0 - 2:LEAD + S0], carried[:, bass.ds(it * 2 + m0, 1), :][:, 0]))
                    w = [vec[:, bass.ds(it * 2 + (F_W + NU * a + m0), 1)] for a in range(3)]
                    b = vec[:, bass.ds(it * 2 + (F_B + m0), 1)]
                    if is_value:
                        dve.wait_ge(s_hl, it * 2)
                        link(ts(dst, u_r[:, 2:2 + T], w[0], b, ALU.mult, ALU.add))
                    else:
                        link(ts(dst, u_r[:, 2:2 + T], w[0], None, ALU.mult))
                    link(stt(dst, u_r[:, 3:3 + T], w[1], dst, ALU.mult, ALU.add))
                    tail = u_r[:, LEAD + T - 72:].rearrange("p (a b) -> p a b", b=36)[:, :, 34:36]
                    out_ = st2[:, :, :].rearrange("p (a b) m -> p m a b", a=2)
                    step.on(nc.vector.tensor_copy(out_[:, bass.ds(it * 2 + m0, 1)][:, 0], tail))
                    stt(dst, u_r[:, 4:4 + T], w[2], dst, ALU.mult, ALU.add).then_inc(s_gc, 1)
                    if is_value:
                        dve.wait_ge(s_gc, it * 4 + (r + 1))
                        dve.wait_ge(s_sg, it * 2 + (j + 1))
                        tt(dst, uct[:, j, :], dst, ALU.mult).then_inc(s_h2, 1)
                        dve.wait_ge(s_hh, it * 2 + (j + 1))
                        tt(one(hl, it * 2 + j, slice(None))[:, 0], dst, one(hh, it * 2 + j, slice(None))[:, 0].bitcast(F32), ALU.subtract).then_inc(s_hl, 1)
            for m in range(KD):
                for q in range(3):
                    t = I_DOWN + 3 * m + q + 2
                    if t < N_ITEMS:
                        split_lo(t, t, min(KD, KF - KD * ((t - I_DOWN) % 3)) * P)
                dve.wait_ge(s_used, I_DOWN + 3 * (m + 1))
                if m >= 2:
                    dve.wait_ge(s_yt, m - 1)
                tt(halves(yT[:, m % 2, :]), pair(m), halves(xT[:, m, :]), ALU.add).then_inc(s_free, 1)

        @block.tensor
        def _(pe):
            mm = nc.tensor.matmul

            def product(x_h, x_l, rank, items):
                total = items[-1][2] + items[-1][3]
                for t, slot, k0, nk in items:
                    pe.wait_ge(s_lo, t + 1)
                    for k in range(nk):
                        cols = slice(k * P, (k + 1) * P)
                        for w, x, first in ((hi, x_h, True), (hi, x_l, False), (lo, x_h, False)):
                            for j in range(2):
                                last = mm(PS[:, 2 * rank + j, 0:HT], w[:, slot % 2, cols], x[:, k0 + k, j * HT:(j + 1) * HT],
                                          start=(k0 + k == 0 and first), stop=(k0 + k == total - 1 and w is lo))
                    last.then_inc(s_used, 1)

            def x_transpose(t):
                n = TOK[t][2]
                pe.wait_ge(s_xt[t], 16)
                if t >= 2:
                    pe.wait_ge(s_xTa, t - 1)
                    pe.wait_ge(s_xTv, t - 1)
                for k in range(KD):
                    last = nc.tensor.transpose(PS[:, 2 * (t % 2) + k // 4, (k % 4) * P:(k % 4) * P + n],
                                               xnat[0:n, t, k * P:(k + 1) * P], ident[0:n, 0:n])
                last.then_inc(s_xTd, 1)

            def x_sums(t):
                c0, _, n = TOK[t]
                pe.wait_ge(s_sq, t + 1)
                dst = PS[:, 4, c0:c0 + n] if t < NT else PS[:, 5, 0:n]
                for k in range(KD):
                    last = mm(dst, ones[:, :], xsq[:, t % 2, k, 0:n], start=(k == 0), stop=(k == KD - 1))
                last.then_inc(s_ss, 1)

            pe.wait_ge(s_ident, 16)
            x_transpose(0)
            for t in range(NTT):
                if t + 1 < NTT:
                    x_transpose(t + 1)
                x_sums(t)
            pe.wait_ge(s_rows, 16 * 14)
            for a, (c0, n) in enumerate(((0, V_N), (V_N, 2 * NU), (V_N + 2 * NU, 2 * NU), (V_N + 4 * NU, 2 * NU))):
                last = nc.tensor.transpose(PS[:, 6, c0:c0 + n], vrows[0:n, a, :], ident[0:n, 0:n])
            last.then_inc(s_vecT, 1)

            pe.wait_ge(s_xl, KD)
            pe.wait_ge(s_ms, 1)
            pe.wait_ge(s_vec, 1)
            for t4 in range(4):
                pe.wait_ge(s_lo, t4 + 1)
                for t, (c0, p0, n) in enumerate(TOK):
                    w0 = c0 - p0
                    for kk in range(2):
                        k = 2 * t4 + kk
                        cols = slice(kk * LAT, (kk + 1) * LAT)
                        for w, x in ((hi, xnh), (hi, xnl), (lo, xnh)):
                            last = mm(PS[:, 3 + t, 0:LAT], x[:, k, w0:w0 + P], w[:, t4 % 2, cols],
                                      start=(k == 0 and w is hi and x is xnh), stop=(k == KD - 1 and w is lo))
                last.then_inc(s_used, 1)

            def products(it, g0, x_h, x_l, after=None):
                for r in range(4):
                    pe.wait_ge(s_free, it * 4 + (g0 + r - 1) if g0 + r else it * 3)
                    product(x_h, x_l, r % 2, [(it * 4 + (I_IN + g0 + r), r, 0, KD)])
                    if after:
                        after(it, r)

            pe.wait_ge(s_nat, 1)
            with pe.Fori(0, 2) as it:
                products(it, G_U, xnh, xnl)

            pe.wait_ge(s_nn, 1)
            pe.wait_ge(s_krr, 2)
            pe.wait_ge(s_nat, NTT)
            for t, (c0, p0, n) in enumerate(TOK):
                if t == 4:
                    pe.wait_ge(s_lte, 1)
                idn = ident[p0:, p0:]
                bank = PS[:, 4 + t % 4, :]
                for a in range(3):
                    nc.tensor.transpose(bank[:, a * P:a * P + n], nat[p0:, t, a * P:(a + 1) * P], idn)
                nc.tensor.transpose(bank[0:QK, 3 * P:3 * P + n], nat[p0:, t, LAT - QK:LAT], idn).then_inc(s_lt, 1)
            pe.wait_ge(s_state, 32)
            pe.wait_ge(s_lte, 2)
            for t in range(PAST // P):
                last = nc.tensor.transpose(PS[:, 5, t * P:(t + 1) * P], past[:, t, 0:P], ident[:, :])
            last.then_inc(s_lt, 1)
            pe.wait_ge(s_lte, 3)
            for t in range(PAST // P):
                last = nc.tensor.transpose(PS[0:QK, 6, t * P:(t + 1) * P], past[:, t, KVL + ROPE - QK:], ident[:, :])
            last.then_inc(s_lt, 1)

            pe.wait_ge(s_uc, KD)
            pe.wait_ge(s_lte, NTT + 2)

            def lru(it, r):
                n = it * 4 + r
                pe.wait_ge(s_lw[r], it * 32 + 32)
                pe.wait_ge(s_lrui, n)
                for a in range(2):
                    for j in range(2):
                        last = mm(PS[:, 4 + 2 * a + j, 0:HT], lruw[:, r, a, :], one(uc, n, slice(j * HT, (j + 1) * HT))[:, 0],
                                  start=True, stop=True)
                last.then_inc(s_lru, 1)

            with pe.Fori(0, 2) as it:
                products(it, G_GA, xnh, xnl, lru)
            with pe.Fori(0, 2) as it:
                products(it, G_GB, xnh, xnl)

            def qkv(q, par):
                pe.wait_ge(s_pw[par], q * 16 + (32 - 16 * par))
                for u in range(8):
                    if u == 0:
                        pe.wait_ge(s_trf, q * 5)
                    if u >= 3:
                        pe.wait_ge(s_pjf, q * 8 + (u - 2))
                    bank = PS[:, u % 3, :]
                    if u < 5:
                        for a in range(2 if u < 4 else 1):
                            t = 2 * u + a
                            k0 = t * P if t < NKT - 1 else NK - P
                            last = mm(bank[:, a * 2 * P:(a + 1) * 2 * P], latT[:, k0:k0 + P], wkv[:, par, :], start=True, stop=True)
                    else:
                        for a in range(2 if u < 7 else 1):
                            c0, p0, n = TOK[2 * (u - 5) + a]
                            for k in range(NQ):
                                last = mm(bank[:, a * 2 * QK:(a + 1) * 2 * QK], cqT[:, k, c0 - p0:c0 - p0 + P], wq[:, par, k, :],
                                          start=(k == 0), stop=(k == NQ - 1))
                    last.then_inc(s_pj, 1)

            def transpose_kq(q, v):
                bank = PS[:, (8 + v) % 3, :]
                if v == 0:
                    pe.wait_ge(s_pjf, q * 8 + 8)
                    pe.wait_ge(s_kn, q + 1)
                if v == 2:
                    pe.wait_ge(s_qr, q + 1)
                if v >= 3:
                    pe.wait_ge(s_trf, q * 5 + (v - 2))
                if v < 2:
                    for a in range(4):
                        last = nc.tensor.transpose(bank[:, a * P:(a + 1) * P],
                                                   Kn[:, 4 * v + a, :, :].rearrange("p h n -> p (h n)"), ident[:, :])
                elif v == 2:
                    nc.tensor.transpose(bank[:, 0:P], Kn[:, NKT - 1, :, :].rearrange("p h n -> p (h n)"), ident[:, :])
                    for h in range(2):
                        last = nc.tensor.transpose(bank[0:QK, P + h * DEC:P + (h + 1) * DEC], Qn[LASTP:, NT, h, :], ident[LASTP:, LASTP:])
                else:
                    for a in range(4):
                        last = nc.tensor.transpose(bank[0:QK, a * P:(a + 1) * P], Qn[:, a, v - 3, :], ident[:, :])
                last.then_inc(s_tr, 1)

            def scores(p, par, n):
                h, t = divmod(n, 4)
                if n < 8:
                    pe.wait_ge(s_e, p * 9 + max(n - 1, 0))
                    w = (t + 1) * P
                    slot = 2 * par + h
                    if n == 0:
                        pe.wait_ge(s_trf, p * 5 + 5)
                    mm(PS[:, 4 + n % 2, 0:w], QT[0:QK + NT, slot, t * P:(t + 1) * P], KT[0:QK + NT, slot, 0:w],
                       start=True, stop=True).then_inc(s_s, 1)
                else:
                    pe.wait_ge(s_e, p * 9 + 8)
                    for h in range(2):
                        slot = 2 * par + h
                        q_s = QT[0:QK, slot, S0:]
                        mm(PS[h * DEC:(h + 1) * DEC, 4, :], q_s, KT[0:QK, slot, SEQ:SEQ + PAST], start=True, stop=True)
                        last = mm(PS[h * DEC:(h + 1) * DEC, 5, 0:DEC], q_s, KT[0:QK, slot, SEQ + PAST:], start=True, stop=True)
                    last.then_inc(s_s, 1)

            def transpose_probs(p, n):
                t = n % 4
                pe.wait_ge(s_pn, p * 9 + (n + 1))
                if n % 2 == 0:
                    pe.wait_ge(s_ptfa, p * 5 + n // 2)
                else:
                    pe.wait_ge(s_ptfv, p * 4 + (n - 1) // 2)
                bank = PS[:, 6 + n % 2, :]
                if n < 8:
                    for a in range(t + 1):
                        last = nc.tensor.transpose(bank[:, a * P:(a + 1) * P], Pn[:, n % 2, a * P:(a + 1) * P], ident[:, :])
                else:
                    R2 = 2 * DEC
                    nc.tensor.transpose(bank[:, 0:P], Ps[:, 0:P], ident[:, :])
                    for a in range(1, 5):
                        k0 = a * P if a < 4 else PAST + DEC - P
                        last = nc.tensor.transpose(bank[:, a * R2:(a + 1) * R2], Ps[0:R2, k0:k0 + P], ident[0:R2, 0:R2])
                last.then_inc(s_pt, 1)

            def values(p, par, n):
                h, t = divmod(n, 4)
                if n % 2 == 0:
                    pe.wait_ge(s_ptfa, p * 5 + (n // 2 + 1))
                else:
                    pe.wait_ge(s_ptfv, p * 4 + ((n - 1) // 2 + 1))
                if n < 8:
                    if n == 0:
                        pe.wait_ge(s_o, p * 2)
                    for a in range(t + 1):
                        last = mm(PS[h * VD:(h + 1) * VD, 3, t * P:(t + 1) * P], V[:, par, a, h, :], PT[:, n % 2, a * P:(a + 1) * P],
                                  start=(a == 0), stop=(a == t))
                else:
                    pe.wait_ge(s_o, p * 2 + 1)
                    for h in range(2):
                        for a in range(5):
                            last = mm(PS[h * VD:(h + 1) * VD, 3, 0:DEC], V[:, par, 4 + a, h, :], PTs[:, a, h * DEC:(h + 1) * DEC],
                                      start=(a == 0), stop=(a == 4))
                last.then_inc(s_pv, 1)

            def attend(p, par, following):
                if following:
                    qkv(p + 1, 1 - par)
                scores(p, par, 0)
                for n in range(9):
                    if n < 8:
                        scores(p, par, n + 1)
                    if n:
                        values(p, par, n - 1)
                    transpose_probs(p, n)
                    if following and n >= 4:
                        transpose_kq(p + 1, n - 4)
                values(p, par, 8)

            pe.wait_ge(s_free, G_OUT)
            pe.wait_ge(s_rope4, 3)
            qkv(0, 0)
            for v in range(5):
                transpose_kq(0, v)
            with pe.Fori(0, 3) as it:
                attend(it * 2, 0, True)
                attend(it * 2 + 1, 1, True)
            attend(6, 0, True)
            attend(7, 1, False)

            pe.wait_ge(s_ml, KD)
            with pe.Fori(0, 2) as it:
                products(it, G_OUT, mxh, mxl)
            pe.wait_ge(s_ss2, KD)
            for j in range(2):
                last = mm(PS[:, 4 + j, 0:HT], ones[:, :], x2ss[:, j * HT:(j + 1) * HT], start=True, stop=True)
            last.then_inc(s_x2t, 1)
            nc.tensor.transpose(PS[0:64, 7, 0:P], st[:, :, :].rearrange("p a b -> p (a b)"), ident[:, :]).then_inc(s_stT, 1)

            pe.wait_ge(s_xl, 2 * KD)
            with pe.Fori(0, NU // 4) as it:
                products(it, G_UP, x2h, x2l)
            pe.wait_ge(s_gc, NU)
            pe.wait_ge(s_stc, 1)
            for a in range(2):
                last = nc.tensor.transpose(PS[0:2 * NU, 7, a * P:(a + 1) * P],
                                           st2[:, 2 * a:2 * a + 2, :].rearrange("p a b -> p (a b)"), ident[:, :])
            last.then_inc(s_stT, 1)

            def y_transpose(m):
                s = m % 2
                pe.wait_ge(s_free, G_DOWN + m + 1)
                if m >= 2:
                    pe.wait_ge(s_yn, 2 * m - 2)
                elif m == 1:
                    pe.wait_ge(s_stc, 2)
                for t, (c0, _, n) in enumerate(TOK):
                    dst = PS[0:n, 4 + 2 * s, t * P:(t + 1) * P] if t < NT else PS[0:n, 5 + 2 * s, 0:P]
                    last = nc.tensor.transpose(dst, yT[:, s, c0:c0 + n], ident[:, :])
                last.then_inc(s_yt, 1)

            pe.wait_ge(s_hl, KF)
            for m in range(KD):
                items = [(I_DOWN + 3 * m + q, 3 * m + q, KD * q, min(KD, KF - KD * q)) for q in range(3)]
                pe.wait_ge(s_free, G_DOWN + m - 1)
                product(hh, hl, m % 2, items)
                if m:
                    y_transpose(m - 1)
            y_transpose(KD - 1)


_INS = ["x_prompt", "x_sample", "cache_kv_latent", "cache_k_rope", "state_lru_h", "state_lru_conv", "state_ffn_conv",
        "g_mix_norm", "w_in", "g_q_a", "w_q_b", "g_kv_a", "w_kv_b", "g_qn", "g_qr", "g_kn", "g_kr",
        "lru_conv_w", "lru_conv_b", "w_rg", "b_rg", "w_ig", "b_ig", "lru_lambda", "w_out", "g_ffn_norm",
        "w_up", "ffn_conv_w", "ffn_conv_b", "w_down"]
_OUTS = [(1, SEQ, D), (1, DEC, D),
         (1, 1, SEQ, KVL), (1, 1, SEQ, ROPE), (1, 1, D), (1, 1, 3, D), (1, 1, 2, 2 * FF),
         (1, 1, DEC, KVL), (1, 1, DEC, ROPE), (1, 1, D), (1, 1, 3, D), (1, 1, 2, 2 * FF)]


def constants():
    inv = (THETA ** (-np.arange(0, ROPE, 2, dtype=np.float32) / ROPE)).astype(np.float32)
    rope = np.zeros((P, NTT, 2 * HR), np.float32)
    for t in range(NTT):
        pos = (np.arange(P) + t * P if t < NT else np.maximum(np.arange(P) - LASTP, 0) + PAST).astype(np.float32)
        ang = pos[:, None] * inv[None, :]
        rope[:, t, 0:HR], rope[:, t, HR:] = np.cos(ang), np.sin(ang)
    kmask, qmask = np.zeros((NT, NK), np.float32), np.zeros((NT, T), np.float32)
    for t in range(NT):
        kmask[t, t * P + CHUNK:(t + 1) * P] = MASKED
        qmask[t, t * P:t * P + CHUNK] = 1.0
    return {"ident": np.eye(P, dtype=np.float32), "rope": rope.reshape(P, -1), "kmask": kmask, "qmask": qmask}


def kernel(**inputs):
    import numpy as _np
    import concourse.bacc as _bacc
    from concourse import mybir as _mybir
    from concourse.bass_utils import run_bass_kernel_spmd as _run

    nc = _bacc.Bacc("TRN2", target_bir_lowering=False, num_devices=1)
    arrays, ins, consts, outs = {}, {}, {}, []
    for name in _INS:
        a = _np.ascontiguousarray(inputs[name])
        arrays[f"in_{name}_dram"] = a
        ins[name] = nc.dram_tensor(f"in_{name}_dram", a.shape, _mybir.dt.from_np(a.dtype), kind="ExternalInput").ap()
    for name, a in constants().items():
        arrays[f"const_{name}_dram"] = a
        consts[name] = nc.dram_tensor(f"const_{name}_dram", a.shape, _mybir.dt.from_np(a.dtype), kind="ExternalInput").ap()
    for n, shape in enumerate(_OUTS):
        outs.append(nc.dram_tensor(f"out_{n}_dram", shape, _mybir.dt.float32, kind="ExternalOutput").ap())
    layer(nc, ins, consts, outs)
    r = _run(nc, [arrays], core_ids=[0])
    return tuple(r.results[0][f"out_{n}_dram"] for n in range(len(_OUTS)))
```

```python
import numpy as np
import concourse.bass as bass
from concourse import mybir
from concourse.alu_op_type import AluOpType as ALU

F32 = mybir.dt.float32
F32R = mybir.dt.float32r
I32 = mybir.dt.int32
ACT = mybir.ActivationFunctionType
X = mybir.AxisListType.X
P = 128

D = 1024
KD = D // P
SEQ, DEC, PAST = 512, 32, 512
CHUNK = 64
NH, NOPE, ROPE, VD = 16, 64, 32, 64
QK = NOPE + ROPE
HR = ROPE // 2
QL, KVL = 256, 128
NQ = QL // P
FF = 2816
KF = FF // P
LAT = QL + KVL + ROPE
EPS = 1e-6
THETA = 10000.0
MASKED = -1e30
SCALE = QK ** -0.5

PAD = 4
S0 = SEQ + PAD
T = S0 + DEC
HT = T // 2
LEAD = 4
NK = SEQ + PAST + DEC
NKT = NK // P + 1
LASTP = P - DEC
NT = SEQ // P
TOK = [(i * P, 0, P) for i in range(NT)] + [(S0, LASTP, DEC)]
NTT = len(TOK)

V_GMIX, V_CW, V_CB, V_BR, V_BI, V_LAM, V_H0, V_CS, V_GFF, V_GQA = 0, 8, 40, 48, 56, 64, 72, 80, 104, 112
V_N = V_GQA + NQ
F_W, F_B, F_S = V_N, V_N + 3 * 44, V_N + 4 * 44
NU = 2 * KF
V_ALL = V_N + 6 * NU

I_LAT, I_IN, I_OUT = 0, 4, 28
I_UP = I_OUT + KD
I_DOWN = I_UP + NU
N_ITEMS = I_DOWN + 3 * KD
G_U, G_GA, G_GB, G_OUT, G_UP = 0, 8, 16, 24, 32
G_DOWN = G_UP + NU
DONE = I_IN + 1
NP_ = NH // 2


class Count:

    def __init__(self, sem):
        self.sem, self.n, self.term = sem, 0, 0

    def on(self, instruction, by=1):
        instruction.then_inc(self.sem, by)
        self.n += by
        return self.value()

    def value(self):
        return self.n + self.term if not isinstance(self.term, int) else self.n


class Loop:

    def __init__(self, eng, trips, counts):
        self.fori, self.trips, self.counts = eng.Fori(0, trips), trips, counts

    def __enter__(self):
        i = self.fori.__enter__()
        for c, per in self.counts:
            c.term, c.start = i * per, c.n
        return i

    def __exit__(self, *a):
        for c, per in self.counts:
            assert c.n - c.start == per, (c.sem, c.n - c.start, per)
            c.n += per * (self.trips - 1)
            c.term = 0
        return self.fori.__exit__(*a)


def layer(nc, i, c, o):
    from contextlib import ExitStack
    ctx = ExitStack()
    with ctx:
        base = 16512

        def at(name, shape, offset, dtype=F32):
            return nc.alloc_sbuf_tensor_at(name, shape, dtype, offset=base + offset)

        XB = KD * T * 4
        place = 0

        def fixed(name, shape, dtype=F32):
            nonlocal place
            n = int(np.prod(shape[1:])) * 4
            t = at(name, shape, place, dtype)
            place += -(-n // 32) * 32
            return t

        ident = fixed("ident", [P, P])
        ones = fixed("ones", [P, P])
        rope = fixed("rope", [P, NTT, 2 * HR])
        bc = fixed("bc", [P, KVL + QK + ROPE])
        gkn = fixed("gkn", [P, 1])
        gqn = fixed("gqn", [P, 1])
        vec = fixed("vec", [P, V_ALL])
        zero = fixed("zero", [P, 4])
        la_s = fixed("la_s", [P, KD])
        small = fixed("small", [P, 8, 40])
        xT = fixed("xT", [P, KD, T])
        rs_at = place
        rsT = fixed("rsT", [P, T])
        raw = fixed("w_raw", [P, 4, KD * P])
        hi = fixed("w_hi", [P, 2, KD * P], F32R)
        lo = fixed("w_lo", [P, 2, KD * P], F32R)
        region = place
        U = fixed("U", [P, KD, LEAD + T])
        sigA = fixed("sigA", [P, KD, T])
        cqT = fixed("cqT", [P, NQ, T])
        latT = fixed("latT", [P, NK])
        kt_at = place
        KT = fixed("KT", [P, 4, NK])
        qt_at = place
        QT = fixed("QT", [P, 4, T])
        xs = place
        xnh = fixed("xnh", [P, KD, T], F32R)
        xnl = fixed("xnl", [P, KD, T], F32R)
        th_at = place
        th = fixed("th", [P, KD, T])
        qs_at = place
        uc = fixed("uc", [P, KD, T])
        tmp_at = place
        tmp = fixed("tmp", [P, 4, T])
        lruw_at = place
        lruw = fixed("lruw", [P, 4, 2, P])
        tmp_end = place
        assert region + D * 4 + 4 * P * 4 + NTT * P * 4 <= region + KD * (LEAD + T) * 4
        xnat = at("xnat", [P, NTT, D], th_at)
        junk = at("junk", [P, D], region)
        junk2 = at("junk2", [P, QL], th_at)
        vrows = at("vrows", [P, 4, P], region + D * 4)
        dgx = at("dgx", [P, NTT, P], region + D * 4 + 4 * P * 4)
        nat = at("nat", [P, NTT, LAT], qt_at)
        past = at("past", [P, PAST // P, KVL + ROPE], kt_at + 3 * NK * 4)
        krot = at("krot", [P, 4, NTT, HR], kt_at + 2 * NK * 4)
        a2 = at("a2", [P, 2, T], qt_at)
        place = th_at
        mxh = at("mxh", [P, KD, T], xs, F32R)
        mxl = at("mxl", [P, KD, T], xs + XB, F32R)
        wq = fixed("wq", [P, 2, NQ, 2 * QK])
        Kn = fixed("Kn", [P, 2, NKT, 2, NOPE])
        Qn = fixed("Qn", [P, 2, NTT, 2, QK])
        V = fixed("V", [P, 2, NKT, 2, VD])
        kqs_at = place
        kqs = fixed("kqs", [P, NKT * 2 * NOPE])
        rot = at("rot", [P, 4, NTT * 2, HR], kqs_at)
        Pn = fixed("Pn", [P, 3, SEQ])
        PT = fixed("PT", [P, 2, SEQ])
        assert place >= lruw_at
        wkv = fixed("wkv", [P, 2, 2, 2 * NOPE])
        dg = at("diag", [P, 3, P], rs_at)
        att_end = place
        place = region
        x2h = fixed("x2h", [P, KD, T], F32R)
        x2l = fixed("x2l", [P, KD, T], F32R)
        hh = fixed("hh", [P, KF, T], F32R)
        hl = fixed("hl", [P, KF, T], F32R)
        upx = fixed("upx", [P, 4, LEAD + T])
        uct = fixed("uct", [P, 4, T])
        stT = fixed("stT", [P, P])
        st2T = fixed("st2T", [P, 2, P])
        ffn_end = place
        sq2 = at("sq2", [P, 2, T], th_at)
        nrm = at("nrm", [P, 2, T], th_at + 2 * T * 4)
        x2ss = at("x2ss", [P, T], th_at + 6 * T * 4)
        assert th_at + 7 * T * 4 <= region + 2 * XB + 2 * KF * T * 4
        place = max(tmp_end, att_end, ffn_end)
        st = fixed("st", [P, 8, KD])
        st2 = fixed("st2", [P, 4, NU])
        ynat = at("ynat", [P, 2, 5, P], region)
        yT = at("yT", [P, 2, T], region + 2 * 5 * P * 4)
        assert base + place <= 229368, base + place

        PS = ctx.enter_context(nc.psum_tensor("PS", [P, 8, 512], F32))

        def pair(g):
            return PS[:, 2 * (g % 2):2 * (g % 2) + 2, 0:HT]

        def halves(ap):
            return ap.rearrange("p (a b) -> p a b", a=2)

        def sem(name):
            return ctx.enter_context(nc.semaphore(name))

        s_ident, s_const, s_rows, s_state = sem("ident_in"), sem("const_in"), sem("rows_in"), sem("past_in")
        s_xt = [sem(f"x{t}_in") for t in range(NTT)]
        s_w = [sem(f"w{s}_in") for s in range(4)]
        s_lw = [sem(f"lruw{s}_in") for s in range(4)]
        s_wkq = [sem(f"pair_wkq{s}_in") for s in range(2)]
        s_wv = [sem(f"pair_wv{s}_in") for s in range(2)]
        s_out, s_lout = sem("stored"), sem("latents_stored")
        s_yout, s_ylast = [sem(f"y{s}_stored") for s in range(2)], sem("last_y_stored")

        s_hi, s_lo, s_used = sem("w_hi_done"), sem("w_lo_done"), sem("w_item_multiplied")
        s_free = sem("product_evacuated")
        s_dve, s_act, s_pool = sem("dve_step"), sem("act_step"), sem("pool_step")
        s_vecT, s_vec = sem("vectors_transposed"), sem("vectors_ready")
        s_xTd, s_xTa, s_xTv = sem("x_transposed"), sem("xT_left_half"), sem("xT_right_half")
        s_ss, s_ms, s_rsg = sem("sums_of_squares"), sem("mean_squares"), sem("rsqrt_guess")
        s_rsn, s_rsb, s_rs = sem("x_rms_inverse"), sem("x_rms_spread"), sem("x_rms_ready")
        s_mask, s_cpre = sem("masks_in"), sem("cleared_first")
        s_xh, s_xl = sem("x_hi"), sem("x_lo")
        s_nat = sem("latent_evacuated")
        s_ns, s_nn, s_krr = sem("latent_squares"), sem("latent_normed"), sem("key_rotated")
        s_lt, s_lte, s_rope4 = sem("latent_transposed"), sem("latent_columns"), sem("key_rope_copied")
        s_uc, s_spe, s_sp = sem("conv_ready"), sem("exp_minus_lambda"), sem("softplus_ready")
        s_lru, s_lrui, s_iu = sem("lru_gates"), sem("lru_gates_read"), sem("lru_gated_input")
        s_a, s_a2, s_m2, s_mult, s_bt = sem("lru_a"), sem("lru_a2"), sem("lru_m2"), sem("lru_mult"), sem("lru_b")
        s_gb, s_rec = sem("sigmoid_b"), sem("gated_recurrence")
        s_stT, s_stc = sem("states_transposed"), sem("states_copied")
        s_clear = sem("cleared")
        s_kq, s_kqf = sem("kq_product"), sem("kq_evacuated")
        s_v, s_vf = sem("v_product"), sem("v_evacuated")
        s_kqs, s_kqm = sem("kq_squares"), sem("kq_mean")
        s_kn, s_qn, s_qr = sem("k_normed"), sem("q_normed"), sem("q_rotated")
        s_tr, s_trf = sem("kq_transposed"), sem("kq_columns")
        s_s, s_mx, s_e, s_dg = sem("scores"), sem("score_max"), sem("exps"), sem("row_inverse")
        s_pt, s_ptf = sem("probs_transposed"), sem("probs_columns")
        s_pv, s_o, s_ml = sem("values"), sem("attn_evacuated"), sem("mixed")
        s_x2q, s_ss2, s_x2t = sem("x2_squares"), sem("x2_squares_added"), sem("x2_sums")
        s_x2z = sem("x2_sums_cleared")
        s_gc, s_sg, s_h2, s_hh, s_hl = sem("gate_conv"), sem("gate_silu"), sem("hidden"), sem("hidden_hi"), sem("hidden_lo")
        s_yt, s_yn = sem("y_transposed"), sem("y_natural")

        block = ctx.enter_context(nc.Block())

        w_in_k = i["w_in"][0].rearrange("(k p) n -> p k n", p=P)
        w_out_k = i["w_out"][0].rearrange("(k p) n -> p k n", p=P)
        w_up_k = i["w_up"][0].rearrange("(k p) n -> p k n", p=P)
        w_down_k = i["w_down"][0].rearrange("(k p) n -> p k n", p=P)
        w_q_k = i["w_q_b"][0].rearrange("(k p) n -> p k n", p=P)
        raw3 = raw[:, :, :].rearrange("p s (k n) -> p s k n", k=KD)

        def after(eng, sem_, value):
            if not isinstance(value, int) or value > 0:
                eng.wait_ge(sem_, value)

        NU_A = 9
        SB = (2, 4, 5)
        HP = PAST // 2
        TILES = (4, 4, 1, 2, 2, 1)
        T_STEPS = {3: (0, 1), 5: (2, 3), 6: (4,)}

        def width(n):
            return (n % 4 + 1) * P if n < 8 else HP + DEC

        def one(t, n, *rest):
            return t[(slice(None), bass.ds(n, 1)) + rest] if not isinstance(n, int) else t[(slice(None), slice(n, n + 1)) + rest]

        @block.sync
        def _(sp):
            sp.dma_start(ident[:, :], c["ident"]).then_inc(s_ident, 16)
            for t, (c0, p0, n) in enumerate(TOK):
                src = i["x_prompt"][0, c0:c0 + n, :] if t < NT else i["x_sample"][0]
                sp.dma_start(xnat[p0:, t, :], src).then_inc(s_xt[t], 16)
            for v0, name, n in ((V_GMIX, "g_mix_norm", 8), (V_CB, "lru_conv_b", 8), (V_BR, "b_rg", 8), (V_BI, "b_ig", 8),
                                (V_LAM, "lru_lambda", 8), (V_H0, "state_lru_h", 8), (V_GFF, "g_ffn_norm", 8), (V_GQA, "g_q_a", NQ)):
                src = i[name][0] if name == "state_lru_h" else i[name]
                sp.dma_start(vrows[v0:v0 + n, 0, :], src.rearrange("a (m p) -> (a m) p", p=P)).then_inc(s_rows, 16)
            sp.dma_start(vrows[V_CW:V_CW + 32, 0, :], i["lru_conv_w"][0].rearrange("j (m p) -> (j m) p", p=P)).then_inc(s_rows, 16)
            sp.dma_start(vrows[V_CS:V_CS + 24, 0, :], i["state_lru_conv"][0, 0].rearrange("j (m p) -> (j m) p", p=P)).then_inc(s_rows, 16)
            fw = i["ffn_conv_w"][0].rearrange("j (m p) -> (j m) p", p=P)
            sp.dma_start(vrows[0:2 * NU, 1, :], fw[0:2 * NU, :]).then_inc(s_rows, 16)
            sp.dma_start(vrows[0:NU, 2, :], fw[2 * NU:3 * NU, :]).then_inc(s_rows, 16)
            sp.dma_start(vrows[NU:2 * NU, 2, :], i["ffn_conv_b"].rearrange("a (m p) -> (a m) p", p=P)).then_inc(s_rows, 16)
            sp.dma_start(vrows[0:2 * NU, 3, :], i["state_ffn_conv"][0, 0].rearrange("j (m p) -> (j m) p", p=P)).then_inc(s_rows, 16)
            for t in range(4):
                sp.dma_start(raw[:, t, 0:2 * LAT].rearrange("p (k n) -> p k n", k=2),
                             w_in_k[:, 2 * t:2 * t + 2, 0:LAT]).then_inc(s_w[t], 16)
            with sp.Fori(0, 6) as it:
                for r in range(4):
                    sp.wait_ge(s_lo, it * 4 + (I_IN + r - 3))
                    sp.dma_start(raw3[:, r], w_in_k[:, :, bass.ds(it * (4 * P) + (LAT + r * P), P)]).then_inc(s_w[r], 16)

            def w_out_items(q):
                for r in range(4):
                    sp.wait_ge(s_lo, q * 4 + (I_OUT + r - 3))
                    sp.dma_start(raw3[:, r], w_out_k[:, :, (4 * q + r) * P:(4 * q + r + 1) * P]).then_inc(s_w[r], 16)

            w_kv_k = i["w_kv_b"][0].rearrange("k (h c n) -> k c h n", c=2, n=NOPE)

            def pair_weights(kind, q, par):
                dst = wkv[:, par, :, :].rearrange("p c (h n) -> p c h n", h=2)
                sem_ = s_wv[par] if kind else s_wkq[par]
                for h in range(2):
                    sp.dma_start(dst[:, kind, h, :], w_kv_k[:, kind, bass.ds(q * 2 + h, 1), :][:, 0]).then_inc(sem_, 16)
                if not kind:
                    sp.dma_start(wq[:, par, :, :], w_q_k[:, :, bass.ds(q * (2 * QK), 2 * QK)]).then_inc(sem_, 16)

            sp.wait_ge(s_lte, NTT + 2)
            for s in range(1, 4):
                sp.dma_start(KT[NOPE:QK, s, :], KT[NOPE:QK, 0, :]).then_inc(s_rope4, 16)
            w_out_items(0)
            sp.wait_ge(s_lrui, KD)
            sp.wait_ge(s_bt, 4)
            for par in range(2):
                for kind in range(2):
                    pair_weights(kind, par, par)
            with sp.Fori(1, NP_ // 2) as it:
                for par in range(2):
                    sp.wait_ge(s_kq, it * 12 + (6 * par - 6))
                    pair_weights(0, it * 2 + par, par)
                    sp.wait_ge(s_v, it * 6 + (3 * par - 3))
                    pair_weights(1, it * 2 + par, par)
            w_out_items(1)
            with sp.Fori(0, NU // 4) as it:
                for r in range(4):
                    sp.wait_ge(s_lo, it * 4 + (I_UP + r - 3))
                    sp.dma_start(raw3[:, r], w_up_k[:, :, bass.ds(it * (2 * P) + ((r // 2) * P + (r % 2) * FF), P)]).then_inc(s_w[r], 16)
            with sp.Fori(0, 2) as it:
                for r in range(12):
                    m, k0 = r // 3, KD * (r % 3)
                    nk = min(KD, KF - k0)
                    sp.wait_ge(s_lo, it * 12 + (I_DOWN + r - 3))
                    sp.dma_start(raw3[:, r % 4, 0:nk], w_down_k[:, k0:k0 + nk, bass.ds(it * (4 * P) + m * P, P)]).then_inc(s_w[r % 4], 16)
            y_p = o[0][0].rearrange("(t p) n -> p t n", p=P)
            for m in range(KD - 2, KD):
                sp.wait_ge(s_yn, 2 * m + 2)
                sp.dma_start(y_p[:, :, m * P:(m + 1) * P], ynat[:, m % 2, 0:NT, :]).then_inc(s_ylast, 16)
                sp.dma_start(o[1][0][:, m * P:(m + 1) * P], ynat[0:DEC, m % 2, NT, :]).then_inc(s_ylast, 16)
            sp.wait_ge(s_ylast, 16 * 4)

        @block.gpsimd
        def _(pool):
            step = Count(s_pool)
            pool.wait_ge(s_xt[NT], 16)
            pool.dma_start(bc[:, 0:KVL], i["g_kv_a"].broadcast_to([P, KVL])).then_inc(s_const, 16)
            pool.dma_start(bc[:, KVL + NOPE:KVL + QK], i["g_qr"].broadcast_to([P, ROPE])).then_inc(s_const, 16)
            pool.dma_start(bc[:, KVL + QK:], i["g_kr"].broadcast_to([P, ROPE])).then_inc(s_const, 16)
            for h in range(2):
                pool.dma_start(gkn[h * NOPE:(h + 1) * NOPE, :], i["g_kn"].rearrange("a p -> p a")).then_inc(s_const, 16)
                pool.dma_start(gqn[h * NOPE:(h + 1) * NOPE, :], i["g_qn"].rearrange("a p -> p a")).then_inc(s_const, 16)
            pool.dma_start(rope[:, :, :], c["rope"].rearrange("p (t n) -> p t n", t=NTT)).then_inc(s_const, 16)
            pool.dma_start(past[:, :, 0:KVL], i["cache_kv_latent"][0, 0].rearrange("(t p) n -> p t n", p=P)).then_inc(s_state, 16)
            pool.dma_start(past[:, :, KVL:], i["cache_k_rope"][0, 0].rearrange("(t p) n -> p t n", p=P)).then_inc(s_state, 16)

            def lru_weights(n):
                pool.dma_start(lruw[:, n % 4, 0, :], i["w_rg"][0, n]).then_inc(s_lw[n % 4], 16)
                pool.dma_start(lruw[:, n % 4, 1, :], i["w_ig"][0, n]).then_inc(s_lw[n % 4], 16)

            for n in range(4):
                lru_weights(n)

            cos, sin = rope[:, :, 0:HR], rope[:, :, HR:]

            def store_latents():
                pool.wait_ge(s_const, 16 * 8)
                pool.wait_ge(s_nn, NTT)
                k1, k2 = nat[:, :, LAT - ROPE:LAT - HR], nat[:, :, LAT - HR:LAT]
                for n, (a, b) in enumerate(((k1, cos), (k2, sin), (k1, sin), (k2, cos))):
                    step.on(nc.gpsimd.tensor_tensor(krot[:, n, :, :], a, b, ALU.mult))
                pool.wait_ge(s_pool, step.value())
                nc.gpsimd.tensor_tensor(k1, krot[:, 0, :, :], krot[:, 1, :, :], ALU.subtract).then_inc(s_krr, 1)
                nc.gpsimd.tensor_tensor(k2, krot[:, 2, :, :], krot[:, 3, :, :], ALU.add).then_inc(s_krr, 1)
                pool.wait_ge(s_krr, 2)
                for c0, n, dst_p, dst_s in ((QL, KVL, o[2], o[7]), (QL + KVL, ROPE, o[3], o[8])):
                    pool.dma_start(dst_p[0, 0].rearrange("(t p) n -> p t n", p=P), nat[:, 0:NT, c0:c0 + n]).then_inc(s_lout, 16)
                    pool.dma_start(dst_s[0, 0], nat[LASTP:P, NT, c0:c0 + n]).then_inc(s_lout, 16)

            for n in range(KD):
                pool.wait_ge(s_lrui, n + 1)
                if n < 4:
                    lru_weights(n + 4)
                nc.gpsimd.tensor_tensor(uc[:, n, :], tmp[:, 2 + n % 2, :], uc[:, n, :], ALU.mult).then_inc(s_iu, 1)
                if n == 4:
                    store_latents()
            pool.wait_ge(s_iu, KD)
            pool.wait_ge(s_lte, NTT + 2)
            pool.wait_ge(s_lout, 64)
            with pool.Fori(0, 2) as it:
                for r in range(4):
                    pool.wait_ge(s_a, it * 4 + (r + 1))
                    pool.wait_ge(s_m2, it * 4 + (r - 1) if r else it * 3)
                    a_n = one(U, it * 4 + r, slice(LEAD, None))[:, 0]
                    nc.gpsimd.tensor_tensor(a2[:, r % 2, :], a_n, a_n, ALU.mult).then_inc(s_a2, 1)
                for r in range(4):
                    pool.wait_ge(s_mult, it * 4 + (r + 1))
                    b_n = one(uc, it * 4 + r, slice(None))[:, 0]
                    nc.gpsimd.tensor_tensor(b_n, one(th, it * 4 + r, slice(None))[:, 0], b_n, ALU.mult).then_inc(s_bt, 1)
            for s in range(4):
                pool.dma_start(KT[QK:QK + NT, s, :], c["kmask"]).then_inc(s_mask, 16)
                pool.dma_start(QT[QK:QK + NT, s, :], c["qmask"]).then_inc(s_mask, 16)

            def squares(q, par):
                kn3 = Kn[:, par, :, :, :].rearrange("p t h n -> p (t h) n")
                qn3 = Qn[:, par, :, :, :].rearrange("p t h n -> p (t h) n")
                pool.wait_ge(s_kqf, q * 6 + 3)
                pool.wait_ge(s_kqm, q * 2)
                pool.wait_ge(s_qr, q)
                nc.gpsimd.tensor_tensor(kqs[:, :].rearrange("p (t n) -> p t n", n=NOPE), kn3, kn3, ALU.mult).then_inc(s_kqs, 1)
                pool.wait_ge(s_kqf, q * 6 + 6)
                pool.wait_ge(s_kqm, q * 2 + 1)
                nc.gpsimd.tensor_tensor(kqs[:, 0:NTT * 2 * QK].rearrange("p (t n) -> p t n", n=QK), qn3, qn3, ALU.mult).then_inc(s_kqs, 1)

            def rotate(q, par):
                q1, q2 = Qn[:, par, :, :, NOPE:NOPE + HR], Qn[:, par, :, :, NOPE + HR:]
                ro = rot[:, :, :, :].rearrange("p f (t h) n -> p f t h n", h=2)
                pool.wait_ge(s_qn, q + 1)
                for h in range(2):
                    for n, (a, b) in enumerate(((q1, cos), (q2, sin), (q1, sin), (q2, cos))):
                        step.on(nc.gpsimd.tensor_tensor(ro[:, n, :, h], a[:, :, h], b, ALU.mult))
                pool.wait_ge(s_pool, step.value())
                for h in range(2):
                    nc.gpsimd.tensor_tensor(q1[:, :, h], ro[:, 0, :, h], ro[:, 1, :, h], ALU.subtract)
                    last = nc.gpsimd.tensor_tensor(q2[:, :, h], ro[:, 2, :, h], ro[:, 3, :, h], ALU.add)
                last.then_inc(s_qr, 1)

            pool.wait_ge(s_rec, KD)
            nc.gpsimd.memset(V[0:LASTP, :, NKT - 1, :, :], 0.0).then_inc(s_clear, 1)
            pool.wait_ge(s_clear, 1)
            with Loop(pool, NP_ // 2, [(step, 16)]) as it:
                for par in range(2):
                    squares(it * 2 + par, par)
                    rotate(it * 2 + par, par)
            pool.wait_ge(s_ml, KD)
            nc.gpsimd.memset(x2ss[:, :], 0.0).then_inc(s_x2z, 1)
            pool.wait_ge(s_x2z, 1)
            with pool.Fori(0, 2) as it:
                for r in range(4):
                    pool.wait_ge(s_x2q, it * 4 + (r + 1))
                    pool.wait_ge(s_ss2, it * 4 + r)
                    nc.gpsimd.tensor_tensor(x2ss[:, :], x2ss[:, :], sq2[:, r % 2, :], ALU.add).then_inc(s_ss2, 1)
            with pool.Fori(0, NU // 4) as it:
                for j in range(2):
                    pool.wait_ge(s_sg, it * 2 + (j + 1))
                    pool.wait_ge(s_gc, it * 4 + (2 * j + 2))
                    nc.gpsimd.tensor_tensor(uct[:, 2 + j, :], uct[:, j, :], uct[:, 2 + j, :], ALU.mult).then_inc(s_h2, 1)
                    pool.wait_ge(s_h2, it * 2 + (j + 1))
                    nc.gpsimd.tensor_copy(one(hh, it * 2 + j, slice(None))[:, 0], uct[:, 2 + j, :]).then_inc(s_hh, 1)
                    pool.wait_ge(s_hh, it * 2 + (j + 1))
                    nc.gpsimd.tensor_tensor(one(hl, it * 2 + j, slice(None))[:, 0], uct[:, 2 + j, :],
                                            one(hh, it * 2 + j, slice(None))[:, 0].bitcast(F32), ALU.subtract).then_inc(s_hl, 1)
            pool.wait_ge(s_stc, 1)
            pool.dma_start(o[4][0].rearrange("a (m p) -> (a m) p", p=P), stT[0:8, :]).then_inc(s_out, 16)
            pool.dma_start(o[9][0].rearrange("a (m p) -> (a m) p", p=P), stT[8:16, :]).then_inc(s_out, 16)
            pool.dma_start(o[5][0, 0].rearrange("j (m p) -> (j m) p", p=P), stT[16:40, :]).then_inc(s_out, 16)
            pool.dma_start(o[10][0, 0].rearrange("j (m p) -> (j m) p", p=P), stT[40:64, :]).then_inc(s_out, 16)
            pool.wait_ge(s_stc, 2)
            pool.dma_start(o[6][0, 0].rearrange("j (m p) -> (j m) p", p=P), st2T[0:2 * NU, 0, :]).then_inc(s_out, 16)
            pool.dma_start(o[11][0, 0].rearrange("j (m p) -> (j m) p", p=P), st2T[0:2 * NU, 1, :]).then_inc(s_out, 16)
            y_p = o[0][0].rearrange("(t p) n -> p t n", p=P)
            for m in range(KD - 2):
                pool.wait_ge(s_yn, 2 * m + 2)
                pool.dma_start(y_p[:, :, m * P:(m + 1) * P], ynat[:, m % 2, 0:NT, :]).then_inc(s_yout[m % 2], 16)
                pool.dma_start(o[1][0][:, m * P:(m + 1) * P], ynat[0:DEC, m % 2, NT, :]).then_inc(s_yout[m % 2], 16)
            pool.wait_ge(s_out, 16 * 6)
            for s in range(2):
                pool.wait_ge(s_yout[s], 16 * (KD - 2))

        @block.scalar
        def _(act):
            step = Count(s_act)

            def link(ins):
                act.wait_ge(s_act, step.on(ins))

            def split_hi(t, slot, loaded, n=KD * P):
                act.wait_ge(s_w[slot % 4], loaded)
                if not isinstance(t, int) or t >= 2:
                    act.wait_ge(s_used, t - 1)
                nc.scalar.activation(hi[:, slot % 2, 0:n], raw[:, slot % 4, 0:n], ACT.Copy).then_inc(s_hi, 1)

            def rsqrt_guess(dst, src, sem_):
                link(nc.scalar.activation(dst, src, ACT.Ln))
                nc.scalar.activation(dst, dst, ACT.Exp, scale=-0.5).then_inc(sem_, 1)

            def xT_left(t):
                c0, _, n = TOK[t]
                act.wait_ge(s_xTd, t + 1)
                nc.scalar.activation(xT[:, 0:4, c0:c0 + n], PS[:, 2 * (t % 2), :].rearrange("p (k n) -> p k n", k=4)[:, :, 0:n],
                                     ACT.Copy).then_inc(s_xTa, 1)

            def x_hi(dst, k, g0):
                nc.scalar.activation(dst[:, k, :], xT[:, k, :], ACT.Copy, scale=vec[:, g0 + k:g0 + k + 1]).then_inc(s_xh, 1)

            for t in range(NTT):
                xT_left(t)
            act.wait_ge(s_vecT, 1)
            nc.scalar.activation(vec[:, 0:V_ALL], PS[:, 6, 0:V_ALL], ACT.Copy).then_inc(s_vec, 1)
            act.wait_ge(s_vec, 1)
            act.wait_ge(s_xTa, NTT)
            act.wait_ge(s_xTv, NTT)
            for k in range(KD):
                x_hi(xnh, k, V_GMIX)
                if k in (1, 3):
                    split_hi(k // 2, k // 2, 16, 2 * LAT)
            act.wait_ge(s_cpre, 1)
            for t, (c0, p0, n) in enumerate(TOK):
                if t:
                    act.wait_ge(s_ss, t)
                nc.scalar.activation(junk[p0:, :], xnat[p0:, t, :], ACT.Square, accum_out=small[p0:, 2, t:t + 1]).then_inc(s_ss, 1)
            nc.scalar.activation(la_s[:, :], vec[:, V_LAM:V_LAM + KD], ACT.Exp, scale=-1.0).then_inc(s_spe, 1)
            for t in range(2, 4):
                split_hi(t, t, 16, 2 * LAT)
            for t in range(4, 6):
                split_hi(t, t, 32)
            act.wait_ge(s_used, I_IN)
            act.wait_ge(s_rsn, 1)
            for t in range(NTT):
                nc.scalar.activation(nat[:, t, :], PS[:, 3 + t, 0:LAT], ACT.Copy, scale=small[:, 3, t:t + 1]).then_inc(s_nat, 1)
            act.wait_ge(s_nat, NTT)
            for t in range(NTT):
                for a, (c0, n) in enumerate(((0, QL), (QL, KVL), (QL + KVL, ROPE))):
                    link(nc.scalar.activation(junk2[:, 0:n], nat[:, t, c0:c0 + n], ACT.Square, accum_out=small[:, 0, a * NTT + t:a * NTT + t + 1]))
            nc.scalar.activation(junk2[:, 0:1], ident[:, 0:1], ACT.Copy).then_inc(s_ns, 1)

            with act.Fori(0, 2) as it:
                for r in range(4):
                    split_hi(it * 4 + (I_IN + r + 2), r + 2, it * 16 + 16 * (2 + (r + 2) // 4))
            with act.Fori(0, 2) as it:
                for r in range(4):
                    n = it * 4 + r
                    split_hi(it * 4 + (I_IN + 8 + r + 2), r + 2, it * 16 + 16 * (4 + (r + 2) // 4))
                    act.wait_ge(s_free, it * 4 + (G_GA + r + 1))
                    g_n = one(sigA, n, slice(None))[:, 0]
                    nc.scalar.activation(g_n, g_n, ACT.Sigmoid)
                    act.wait_ge(s_lru, n + 1)
                    u_n = one(U, n, slice(LEAD, None))[:, 0]
                    nc.scalar.activation(halves(u_n), PS[:, 4:6, 0:HT], ACT.Sigmoid, bias=vec[:, bass.ds(it * 4 + (V_BR + r), 1)]).then_inc(s_act, 1)
                    act.wait_ge(s_iu, it * 4 + (r - 1) if r else it * 3)
                    nc.scalar.activation(halves(tmp[:, 2 + r % 2, :]), PS[:, 6:8, 0:HT], ACT.Sigmoid, bias=vec[:, bass.ds(it * 4 + (V_BI + r), 1)]).then_inc(s_lrui, 1)
                    act.wait_ge(s_act, it * 8 + (step.n + 2 * r + 1))
                    if r == 0:
                        act.wait_ge(s_sp, 1)
                    nc.scalar.activation(one(th, n, slice(None))[:, 0], u_n, ACT.Tanh, scale=la_s[:, bass.ds(n, 1)]).then_inc(s_act, 1)
            step.n += 16
            act.wait_ge(s_act, step.n)
            with act.Fori(0, 2) as it:
                for r in range(4):
                    if r == 0:
                        for n in range(4):
                            a_n = one(U, it * 4 + n, slice(LEAD, None))[:, 0]
                            nc.scalar.activation(a_n, a_n, ACT.Exp, scale=la_s[:, bass.ds(it * 4 + n, 1)]).then_inc(s_a, 1)
                    split_hi(it * 4 + (I_IN + 16 + r + 2), r + 2, it * 16 + 16 * (6 + (r + 2) // 4))
                    if r == 0:
                        for n in range(4):
                            act.wait_ge(s_m2, it * 4 + (n + 1))
                            m_n = one(th, it * 4 + n, slice(None))[:, 0]
                            nc.scalar.activation(m_n, m_n, ACT.Sqrt, scale=-1.0).then_inc(s_mult, 1)
                for r in range(4):
                    act.wait_ge(s_free, it * 4 + (G_GB + r + 1))
                    nc.scalar.activation(tmp[:, r, :], tmp[:, r, :], ACT.Sigmoid).then_inc(s_gb, 1)

            def evacuate(q, par, u):
                bank = PS[:, u % 2 if u < 6 else (u + 1) % 2, :]
                if u < 6:
                    if u == 0:
                        after(act, s_tr, q * 5 - 5)
                    act.wait_ge(s_kq, q * 6 + (u + 1))
                    tiles = TILES[u]
                    if u < 3:
                        dst = Kn[:, par, 4 * u:4 * u + tiles, :, :].rearrange("p t h n -> p (t h n)")
                        nc.scalar.activation(dst, bank[:, 0:tiles * P], ACT.Copy).then_inc(s_kqf, 1)
                    else:
                        t0 = 2 * (u - 3)
                        dst = Qn[:, par, t0:t0 + tiles, :, :].rearrange("p t h n -> p (t h n)")
                        nc.scalar.activation(dst, bank[:, 0:tiles * 2 * QK], ACT.Copy).then_inc(s_kqf, 1)
                else:
                    u -= 6
                    if u == 0:
                        after(act, s_pv, q * 9 - 9)
                    act.wait_ge(s_v, q * 3 + (u + 1))
                    tiles, p0 = (4, 0) if u < 2 else (1, LASTP)
                    dst = V[p0:, par, 4 * u:4 * u + tiles, :, :].rearrange("p t h n -> p (t h n)")
                    nc.scalar.activation(dst, bank[p0:, 0:tiles * P], ACT.Copy).then_inc(s_vf, 1)

            def exps(p, n, reused):
                act.wait_ge(s_mx, p * 9 + (n + 1))
                after(act, s_pt, p * 9 + (n - 2 if reused else max(n - 2, 0)))
                bank, sm = PS[:, SB[n % 3], :], small[:, 4 + n % 3, :]
                if n < 8:
                    w = width(n)
                    nc.scalar.activation(Pn[:, n % 3, 0:w], bank[:, 0:w], ACT.Exp, bias=sm[:, 2:3],
                                         accum_out=sm[:, 0:1]).then_inc(s_e, 1)
                else:
                    R2 = 2 * DEC
                    nc.scalar.activation(Pn[:, 2, 0:HP], bank[:, 0:HP], ACT.Exp, bias=sm[:, 2:3], accum_out=sm[:, 6:7])
                    nc.scalar.activation(Pn[0:R2, 2, HP:HP + DEC], bank[0:R2, HP:HP + DEC], ACT.Exp, bias=sm[0:R2, 2:3],
                                         accum_out=sm[0:R2, 7:8]).then_inc(s_e, 1)

            def probs_columns(p, par, n):
                act.wait_ge(s_pt, p * 9 + (n + 1))
                after(act, s_pv, p * 9 + max(n - 1, 0))
                b = (n + par) % 2
                w = width(n) if n < 8 else 2 * P + 2 * DEC
                nc.scalar.activation(PT[:, b, 0:w], PS[:, 6 + b, 0:w], ACT.Copy).then_inc(s_ptf, 1)

            def attend(p, par):
                kq = not isinstance(p, int) or p + 2 < NP_
                following = not isinstance(p, int) or p + 1 < NP_
                for n in range(9):
                    if n < 8:
                        exps(p, n + 1, False)
                    elif following:
                        exps(p + 1, 0, True)
                    if kq and n < 3:
                        evacuate(p + 2, par, 2 * n)
                        evacuate(p + 2, par, 2 * n + 1)
                    probs_columns(p, par, n)
                    if following and n == 6:
                        evacuate(p + 1, 1 - par, 6)
                if following:
                    evacuate(p + 1, 1 - par, 7)
                    evacuate(p + 1, 1 - par, 8)

            act.wait_ge(s_bt, KD)
            act.wait_ge(s_rec, 4)
            for q in range(2):
                for u in range(6):
                    evacuate(q, q, u)
            act.wait_ge(s_clear, 1)
            for u in range(6, 9):
                evacuate(0, 0, u)
            exps(0, 0, False)
            with act.Fori(0, 3) as it:
                attend(it * 2, 0)
                attend(it * 2 + 1, 1)
            attend(6, 0)
            attend(7, 1)

            with act.Fori(0, 2) as it:
                for r in range(4):
                    m = it * 4 + r
                    act.wait_ge(s_ss2, it * 4 + (r - 1) if r else it * 3)
                    act.wait_ge(s_free, it * 4 + (G_OUT + r + 1))
                    x_m = one(xT, m, slice(None))[:, 0]
                    nc.scalar.activation(one(x2h, m, slice(None))[:, 0], x_m, ACT.Copy,
                                         scale=vec[:, bass.ds(it * 4 + (V_GFF + r), 1)]).then_inc(s_xh, 1)
                    x_m = one(xT, m, slice(None))[:, 0]
                    split_hi(it * 4 + (I_OUT + r + 2), r + 2, it * 16 + 16 * (8 + (r + 2) // 4))
                    nc.scalar.activation(sq2[:, r % 2, :], x_m, ACT.Square).then_inc(s_x2q, 1)
            act.wait_ge(s_ms, 1)
            rsqrt_guess(rsT[:, :], nrm[:, 0, :], s_rsg)
            act.wait_ge(s_stT, 1)
            nc.scalar.activation(stT[0:64, :], PS[0:64, 7, 0:P], ACT.Copy).then_inc(s_stc, 1)

            with act.Fori(0, NU // 4) as it:
                for r in range(4):
                    split_hi(it * 4 + (I_UP + r + 2), r + 2, it * 16 + 16 * (10 + (r + 2) // 4))
                    if r % 2 == 1:
                        j = r // 2
                        act.wait_ge(s_gc, it * 4 + r)
                        nc.scalar.activation(uct[:, j, :], uct[:, j, :], ACT.Silu,
                                             bias=vec[:, bass.ds(it * 2 + (F_B + j), 1)]).then_inc(s_sg, 1)

            def y_natural(m, s):
                act.wait_ge(s_yt, m + 1)
                act.wait_ge(s_yout[s], 32 * (m // 2))
                nc.scalar.activation(ynat[:, s, 0:NT, :], PS[:, 4 + 2 * s, :].rearrange("p (a b) -> p a b", a=NT), ACT.Copy).then_inc(s_yn, 1)
                nc.scalar.activation(ynat[0:DEC, s, NT, :], PS[0:DEC, 5 + 2 * s, 0:P], ACT.Copy).then_inc(s_yn, 1)

            for m in range(KD):
                for q in range(3):
                    t = I_DOWN + 3 * m + q + 2
                    if t < N_ITEMS:
                        split_hi(t, t, 16 * (t // 4 + 1), min(KD, KF - KD * ((t - I_DOWN) % 3)) * P)
                if m == 0:
                    act.wait_ge(s_stT, 2)
                    st_rows = PS[0:2 * NU, 7, 0:2 * P].rearrange("p (a b) -> p a b", a=2)
                    nc.scalar.activation(st2T[0:2 * NU, :, :], st_rows, ACT.Copy).then_inc(s_stc, 1)
                else:
                    y_natural(m - 1, (m - 1) % 2)
            y_natural(KD - 1, (KD - 1) % 2)

        @block.vector
        def _(dve):
            step = Count(s_dve)
            tt, ts, stt = nc.vector.tensor_tensor, nc.vector.tensor_scalar, nc.vector.scalar_tensor_tensor

            def link(ins):
                dve.wait_ge(s_dve, step.on(ins))

            def split_lo(t, slot, n=KD * P):
                dve.wait_ge(s_hi, t + 1)
                tt(lo[:, slot % 2, 0:n], raw[:, slot % 4, 0:n], hi[:, slot % 2, 0:n].bitcast(F32), ALU.subtract).then_inc(s_lo, 1)

            def newton(y, v, t):
                link(stt(t, y, -0.5, y, ALU.mult, ALU.mult))
                link(tt(t, t, v, ALU.mult))
                link(stt(y, t, 1.5, y, ALU.add, ALU.mult))

            def rsqrt(y, v, t):
                link(ts(y.bitcast(I32), v.bitcast(I32), -0.5, float(0x5F3759DF), ALU.mult, ALU.add))
                for _ in range(3):
                    newton(y, v, t)

            nc.vector.memset(xT[:, :, SEQ:S0], 0.0)
            nc.vector.memset(cqT[:, :, SEQ:S0], 0.0)
            nc.vector.memset(ones[:, :], 1.0)
            nc.vector.memset(zero[:, :], 0.0)
            nc.vector.memset(rsT[:, SEQ:S0], 1.0)
            nc.vector.memset(small[0:LASTP, 2, NT:NTT], 1.0).then_inc(s_cpre, 1)

            for t, (c0, _, n) in enumerate(TOK):
                dve.wait_ge(s_xTd, t + 1)
                nc.vector.tensor_copy(xT[:, 4:8, c0:c0 + n], PS[:, 2 * (t % 2) + 1, :].rearrange("p (k n) -> p k n", k=4)[:, :, 0:n]).then_inc(s_xTv, 1)

            def x_lo(high, low, k, g0, count):
                dve.wait_ge(s_xh, count + k + 1)
                stt(low[:, k, :], xT[:, k, :], vec[:, g0 + k:g0 + k + 1], high[:, k, :].bitcast(F32), ALU.mult, ALU.subtract).then_inc(s_xl, 1)

            for k in range(KD):
                x_lo(xnh, xnl, k, V_GMIX, 0)
                if k in (1, 3):
                    split_lo(k // 2, k // 2, 2 * LAT)
            dve.wait_ge(s_ss, NTT)
            link(ts(small[:, 2, 0:NTT], small[:, 2, 0:NTT], 1.0 / D, EPS, ALU.mult, ALU.add))
            rsqrt(small[:, 3, 0:NTT], small[:, 2, 0:NTT], small[:, 3, 8:8 + NTT])
            for t in range(NTT):
                last = ts(dgx[:, t, :], ident[:, :], small[:, 3, t:t + 1], None, ALU.mult)
            last.then_inc(s_rsn, 1)
            for t in range(2, 4):
                split_lo(t, t, 2 * LAT)
            dve.wait_ge(s_rsb, 1)
            nc.vector.tensor_copy(rsT[:, 0:SEQ], PS[:, 0, :])
            nc.vector.tensor_copy(rsT[:, S0:], PS[:, 1, 0:DEC]).then_inc(s_rs, 1)
            for t in range(4, 6):
                split_lo(t, t)
            dve.wait_ge(s_spe, 1)
            e, q, q2, acc, mxl_ = (small[:, 4 + n // 4, 8 * (n % 4):8 * (n % 4) + 8] for n in range(5))
            lam = vec[:, V_LAM:V_LAM + KD]
            link(nc.vector.reciprocal(q, la_s[:, :]))
            link(tt(e, la_s[:, :], q, ALU.min))
            link(ts(q, e, 2.0, None, ALU.add))
            link(nc.vector.reciprocal(q2, q))
            link(tt(q, e, q2, ALU.mult))
            link(tt(q2, q, q, ALU.mult))
            link(ts(acc, q2, 1.0 / 19, 1.0 / 17, ALU.mult, ALU.add))
            for d in (15, 13, 11, 9, 7, 5, 3, 1):
                link(tt(acc, acc, q2, ALU.mult))
                link(ts(acc, acc, 1.0 / d, None, ALU.add))
            link(tt(acc, acc, q, ALU.mult))
            link(ts(mxl_, lam, -1.0, 0.0, ALU.mult, ALU.max))
            link(stt(acc, acc, 2.0, mxl_, ALU.mult, ALU.add))
            ts(la_s[:, :], acc, -8.0, None, ALU.mult).then_inc(s_sp, 1)

            nc.vector.memset(U[:, :, 0:LEAD], 0.0).then_inc(s_dve, 1)
            step.n += 1
            with Loop(dve, 2, [(step, 20)]) as it:
                for r in range(4):
                    n = it * 4 + r
                    u_n = one(U, n, slice(None))[:, 0]
                    c_n = one(uc, n, slice(None))[:, 0]
                    dve.wait_ge(s_used, it * 4 + (G_U + r + DONE))
                    tt(halves(u_n[:, LEAD:]), pair(r), halves(rsT[:, :]), ALU.mult).then_inc(s_free, 1)
                    split_lo(it * 4 + (I_IN + r + 2), r + 2)
                    dve.wait_ge(s_free, it * 4 + (G_U + r + 1))
                    carried = vec[:, V_CS:V_CS + 24].rearrange("p (j m) -> p m j", j=3)
                    link(nc.vector.tensor_copy(u_n[:, LEAD + S0 - 3:LEAD + S0], carried[:, bass.ds(n, 1), :][:, 0]))
                    w = [vec[:, bass.ds(it * 4 + (V_CW + 8 * j + r), 1)] for j in range(4)]
                    b = vec[:, bass.ds(it * 4 + (V_CB + r), 1)]
                    link(ts(c_n, u_n[:, 1:1 + T], w[0], b, ALU.mult, ALU.add))
                    for j in (1, 2):
                        link(stt(c_n, u_n[:, 1 + j:1 + j + T], w[j], c_n, ALU.mult, ALU.add))
                    step.on(stt(c_n, u_n[:, 4:4 + T], w[3], c_n, ALU.mult, ALU.add))
                    tail = u_n[:, LEAD + T - 72:].rearrange("p (a b) -> p a b", b=36)[:, :, 33:36]
                    out_ = st[:, 2:8, :].rearrange("p (a b) m -> p m a b", a=2)
                    nc.vector.tensor_copy(out_[:, bass.ds(n, 1)][:, 0], tail).then_inc(s_uc, 1)

            def latent_norms():
                dve.wait_ge(s_ns, 1)
                dve.wait_ge(s_const, 16 * 8)
                link(ts(bc[:, KVL + NOPE:KVL + QK], bc[:, KVL + NOPE:KVL + QK], SCALE, None, ALU.mult))
                link(stt(gkn[:, :], gkn[:, :], SCALE, gqn[:, :], ALU.mult, ALU.mult))
                for a, n in enumerate((QL, KVL, ROPE)):
                    ms = small[:, 0, a * NTT:(a + 1) * NTT]
                    link(ts(ms, ms, 1.0 / n, EPS, ALU.mult, ALU.add))
                rsqrt(small[:, 1, 0:3 * NTT], small[:, 0, 0:3 * NTT], small[:, 2, 0:3 * NTT])

            def latent_tile(t):
                rs = [small[:, 1, a * NTT + t:a * NTT + t + 1] for a in range(3)]
                ts(nat[:, t, 0:QL], nat[:, t, 0:QL], rs[0], None, ALU.mult)
                stt(nat[:, t, QL:QL + KVL], nat[:, t, QL:QL + KVL], rs[1], bc[:, 0:KVL], ALU.mult, ALU.mult)
                stt(nat[:, t, QL + KVL:], nat[:, t, QL + KVL:], rs[2], bc[:, KVL + QK:], ALU.mult, ALU.mult).then_inc(s_nn, 1)

            for r in range(KD):
                dve.wait_ge(s_used, G_GA + r + DONE)
                tt(halves(sigA[:, r, :]), pair(r), halves(rsT[:, :]), ALU.mult).then_inc(s_free, 1)
                split_lo(I_IN + 8 + r + 2, r + 2)
                if r == 0:
                    latent_norms()
                elif r < 4:
                    for t in range(2 * r - 2, min(2 * r, NTT)):
                        latent_tile(t)

            dve.wait_ge(s_lt, 1)
            nc.vector.tensor_copy(latT[:, SEQ:SEQ + PAST], PS[:, 0, :]).then_inc(s_lte, 1)
            dve.wait_ge(s_lt, 2)
            nc.vector.tensor_copy(KT[NOPE:QK, 0, SEQ:SEQ + PAST], PS[NOPE:QK, 1, :]).then_inc(s_lte, 1)
            for t, (c0, _, n) in enumerate(TOK):
                dve.wait_ge(s_lt, t + 3)
                bank = PS[:, 4 + t if t < NT else 2, :]
                for a in range(NQ):
                    ts(cqT[:, a, c0:c0 + n], bank[:, a * P:a * P + n], vec[:, V_GQA + a:V_GQA + a + 1], None, ALU.mult)
                k0 = c0 if t < NT else SEQ + PAST
                nc.vector.tensor_copy(latT[:, k0:k0 + n], bank[:, 2 * P:2 * P + n])
                nc.vector.tensor_copy(KT[NOPE:QK, 0, k0:k0 + n], bank[NOPE:QK, 3 * P:3 * P + n]).then_inc(s_lte, 1)

            dve.wait_ge(s_iu, KD)
            with Loop(dve, 2, [(step, 10)]) as it:
                for r in range(4):
                    dve.wait_ge(s_used, it * 4 + (G_GB + r + DONE))
                    if r == 0:
                        dve.wait_ge(s_rec, it * 4)
                    tt(halves(tmp[:, r, :]), pair(r), halves(rsT[:, :]), ALU.mult).then_inc(s_free, 1)
                    split_lo(it * 4 + (I_IN + 16 + r + 2), r + 2)
                    if r == 0:
                        for n in range(4):
                            m_n = one(th, it * 4 + n, slice(None))[:, 0]
                            dve.wait_ge(s_a2, it * 4 + (n + 1))
                            stt(m_n, a2[:, n % 2, :], 1.0, m_n, ALU.add, ALU.mult).then_inc(s_m2, 1)
                    if r == 2:
                        dve.wait_ge(s_bt, it * 4 + 4)
                        link(nc.vector.tensor_copy(U[:, bass.ds(it * 4, 4), LEAD + S0 - 1:LEAD + S0], zero[:, :].unsqueeze(2)))
                        link(nc.vector.tensor_copy(uc[:, bass.ds(it * 4, 4), S0 - 1:S0], vec[:, bass.ds(it * 4 + V_H0, 4)].unsqueeze(2)))
                    if r >= 2:
                        for q in (2 * r - 4, 2 * r - 3):
                            n = it * 4 + q
                            a_n = one(U, n, slice(LEAD, None))[:, 0]
                            link(nc.vector.tensor_tensor_scan(a_n, a_n, one(uc, n, slice(None))[:, 0], 0.0, ALU.mult, ALU.add))
                            ends = a_n[:, T - 72:].rearrange("p (a b) -> p a b", b=36)[:, :, 35:36]
                            link(nc.vector.tensor_copy(st[:, 0:2, bass.ds(n, 1)], ends))
                for r in range(4):
                    a_n = one(U, it * 4 + r, slice(LEAD, None))[:, 0]
                    dve.wait_ge(s_gb, it * 4 + (r + 1))
                    tt(a_n, a_n, tmp[:, r, :], ALU.mult).then_inc(s_rec, 1)

            sq3 = kqs[:, :].rearrange("p (t n) -> p t n", n=NOPE)
            sq4 = kqs[:, 0:NTT * 2 * QK].rearrange("p (t n) -> p t n", n=QK)
            NKH, NQH = 2 * NKT, 2 * NTT
            R2 = 2 * DEC

            def key_sums(q):
                dve.wait_ge(s_kqs, q * 2 + 1)
                nc.vector.tensor_reduce(small[:, 0, 0:NKH], sq3, X, ALU.add).then_inc(s_kqm, 1)

            def query_sums(q):
                dve.wait_ge(s_kqs, q * 2 + 2)
                nc.vector.tensor_reduce(small[:, 0, NKH:NKH + NQH], sq4[:, :, 0:NOPE], X, ALU.add)
                link(nc.vector.tensor_reduce(small[:, 0, NKH + NQH:NKH + 2 * NQH], sq4[:, :, NOPE:], X, ALU.add))
                ts(small[:, 0, 0:NKH + NQH], small[:, 0, 0:NKH + NQH], 1.0 / NOPE, EPS, ALU.mult, ALU.add)
                ts(small[:, 0, NKH + NQH:NKH + 2 * NQH], small[:, 0, NKH + NQH:NKH + 2 * NQH], 1.0 / ROPE, EPS,
                   ALU.mult, ALU.add).then_inc(s_kqm, 1)

            def normalise_keys(q, par):
                kn3 = Kn[:, par, :, :, :].rearrange("p t h n -> p (t h) n")
                dve.wait_ge(s_kqm, q * 2 + 2)
                rsqrt(small[:, 1, 0:38], small[:, 0, 0:38], small[:, 2, 0:38])
                y = small[:, 1, :].unsqueeze(2)
                tt(kn3, kn3, y[:, 0:NKH].to_broadcast([P, NKH, NOPE]), ALU.mult).then_inc(s_kn, 1)

            def normalise_queries(q, par):
                qn3 = Qn[:, par, :, :, :].rearrange("p t h n -> p (t h) n")
                y = small[:, 1, :].unsqueeze(2)
                link(tt(qn3[:, :, NOPE:], qn3[:, :, NOPE:], y[:, NKH + NQH:NKH + 2 * NQH].to_broadcast([P, NQH, ROPE]), ALU.mult))
                tt(qn3[:, :, NOPE:], qn3[:, :, NOPE:], bc[:, KVL + NOPE:KVL + QK].unsqueeze(1).to_broadcast([P, NQH, ROPE]), ALU.mult)
                tt(qn3[:, :, 0:NOPE], qn3[:, :, 0:NOPE], y[:, NKH:NKH + NQH].to_broadcast([P, NQH, NOPE]), ALU.mult).then_inc(s_qn, 1)

            def columns(q, par, v):
                bank = PS[:, v % 2, :]
                dve.wait_ge(s_tr, q * 5 + (v + 1))
                if v < 3:
                    k0, c0, n = (v * 512, 0, 512) if v < 2 else (SEQ + PAST, LASTP, DEC)
                    for h in range(2):
                        ins = ts(KT[0:NOPE, 2 * par + h, k0:k0 + n], bank[h * NOPE:(h + 1) * NOPE, c0:c0 + n],
                                 gkn[h * NOPE:(h + 1) * NOPE, :], None, ALU.mult)
                        if v == 2:
                            ins = nc.vector.tensor_copy(QT[0:QK, 2 * par + h, S0:], bank[0:QK, P + h * DEC:P + (h + 1) * DEC])
                else:
                    ins = nc.vector.tensor_copy(QT[0:QK, 2 * par + v - 3, 0:SEQ], bank[0:QK, :])
                ins.then_inc(s_trf, 1)

            def row_max(p, n):
                dve.wait_ge(s_s, p * 9 + (n + 1))
                bank, sm = PS[:, SB[n % 3], :], small[:, 4 + n % 3, :]
                if n < 8:
                    nc.vector.tensor_reduce(sm[:, 2:3], bank[:, 0:width(n)], X, ALU.max, negate=True).then_inc(s_mx, 1)
                else:
                    link(nc.vector.tensor_reduce(sm[:, 3:4], bank[:, 0:HP], X, ALU.max, negate=True))
                    nc.vector.tensor_reduce(sm[0:R2, 4:5], bank[0:R2, HP:HP + DEC], X, ALU.max, negate=True)
                    link(nc.vector.tensor_copy(sm[0:R2, 5:6], sm[R2:, 3:4]))
                    link(tt(sm[0:R2, 2:3], sm[0:R2, 3:4], sm[0:R2, 4:5], ALU.min))
                    link(tt(sm[0:R2, 2:3], sm[0:R2, 2:3], sm[0:R2, 5:6], ALU.min))
                    nc.vector.tensor_copy(sm[R2:, 2:3], sm[0:R2, 2:3]).then_inc(s_mx, 1)

            def row_inverse(p, n):
                dve.wait_ge(s_e, p * 9 + (n + 1))
                sm = small[:, 4 + n % 3, :]
                if n < 8:
                    link(nc.vector.reciprocal(sm[:, 1:2], sm[:, 0:1]))
                else:
                    nc.vector.tensor_copy(sm[0:R2, 8:9], sm[R2:, 6:7])
                    link(tt(sm[0:R2, 0:1], sm[0:R2, 6:7], sm[0:R2, 7:8], ALU.add))
                    link(tt(sm[0:R2, 0:1], sm[0:R2, 0:1], sm[0:R2, 8:9], ALU.add))
                    link(nc.vector.reciprocal(sm[0:R2, 1:2], sm[0:R2, 0:1]))
                    link(nc.vector.tensor_copy(sm[R2:, 1:2], sm[0:R2, 1:2]))
                ts(dg[:, n % 3, :], ident[:, :], sm[:, 1:2], None, ALU.mult).then_inc(s_dg, 1)

            def attend(p, par):
                kq = not isinstance(p, int) or p + 2 < NP_
                following = not isinstance(p, int) or p + 1 < NP_
                for n in range(9):
                    if n < 7:
                        row_max(p, n + 2)
                    elif following:
                        row_max(p + 1, n - 7)
                    if n < 8:
                        row_inverse(p, n + 1)
                    elif following:
                        row_inverse(p + 1, 0)
                    if following:
                        for v in T_STEPS.get(n, ()):
                            columns(p + 1, 1 - par, v)
                    if kq and n == 6:
                        key_sums(p + 2)
                    if kq and n == 8:
                        query_sums(p + 2)
                    if following and n == 0:
                        normalise_keys(p + 1, 1 - par)
                    if following and n == 1:
                        normalise_queries(p + 1, 1 - par)
                a_p, u_p = one(sigA, p, slice(None))[:, 0], one(U, p, slice(LEAD, None))[:, 0]
                h_p, l_p = one(mxh, p, slice(None))[:, 0], one(mxl, p, slice(None))[:, 0]
                dve.wait_ge(s_pv, p * 9 + 8)
                tt(a_p[:, 0:SEQ], PS[:, 3, :], a_p[:, 0:SEQ], ALU.mult).then_inc(s_o, 1)
                dve.wait_ge(s_pv, p * 9 + 9)
                tt(a_p[:, S0:], PS[:, 6 + par, SEQ - DEC:SEQ], a_p[:, S0:], ALU.mult).then_inc(s_o, 1)
                dve.wait_ge(s_o, p * 2 + 2)
                link(tt(a_p, a_p, u_p, ALU.add))
                link(nc.vector.tensor_copy(h_p, a_p))
                tt(l_p, a_p, h_p.bitcast(F32), ALU.subtract).then_inc(s_ml, 1)

            key_sums(0)
            query_sums(0)
            normalise_keys(0, 0)
            normalise_queries(0, 0)
            dve.wait_ge(s_rope4, 48)
            for v in range(5):
                columns(0, 0, v)
            row_max(0, 0)
            row_max(0, 1)
            row_inverse(0, 0)
            key_sums(1)
            query_sums(1)
            with Loop(dve, 3, [(step, 2 * (1 + 11 + 4 + 8 + 4 + 2))]) as it:
                attend(it * 2, 0)
                attend(it * 2 + 1, 1)
            attend(6, 0)
            attend(7, 1)

            with dve.Fori(0, 2) as it:
                for r in range(4):
                    m = it * 4 + r
                    x_m = one(xT, m, slice(None))[:, 0]
                    dve.wait_ge(s_used, it * 4 + (G_OUT + r + DONE))
                    tt(halves(x_m), pair(r), halves(x_m), ALU.add).then_inc(s_free, 1)
                    dve.wait_ge(s_xh, it * 4 + (KD + r + 1))
                    stt(one(x2l, m, slice(None))[:, 0], x_m, vec[:, bass.ds(it * 4 + (V_GFF + r), 1)],
                        one(x2h, m, slice(None))[:, 0].bitcast(F32), ALU.mult, ALU.subtract).then_inc(s_xl, 1)
                    split_lo(it * 4 + (I_OUT + r + 2), r + 2)
            nc.vector.memset(upx[:, :, 0:LEAD], 0.0)
            dve.wait_ge(s_x2t, 1)
            ts(halves(nrm[:, 0, :]), PS[:, 4:6, 0:HT], 1.0 / D, EPS, ALU.mult, ALU.add).then_inc(s_ms, 1)
            dve.wait_ge(s_rsg, 1)
            newton(rsT[:, :], nrm[:, 0, :], nrm[:, 1, :])

            with Loop(dve, NU // 4, [(step, 16)]) as it:
                for r in range(4):
                    j, is_value = divmod(r, 2)
                    u_r = upx[:, r, :]
                    dst = uct[:, 2 * is_value + j, :]
                    m0 = j + KF * is_value
                    dve.wait_ge(s_used, it * 4 + (G_UP + r + DONE))
                    tt(halves(u_r[:, LEAD:]), pair(r), halves(rsT[:, :]), ALU.mult).then_inc(s_free, 1)
                    split_lo(it * 4 + (I_UP + r + 2), r + 2)
                    dve.wait_ge(s_free, it * 4 + (G_UP + r + 1))
                    carried = vec[:, F_S:F_S + 2 * NU].rearrange("p (s m) -> p m s", s=2)
                    link(nc.vector.tensor_copy(u_r[:, LEAD + S0 - 2:LEAD + S0], carried[:, bass.ds(it * 2 + m0, 1), :][:, 0]))
                    w = [vec[:, bass.ds(it * 2 + (F_W + NU * a + m0), 1)] for a in range(3)]
                    b = vec[:, bass.ds(it * 2 + (F_B + m0), 1)]
                    if r == 0:
                        dve.wait_ge(s_hl, it * 2)
                    link(ts(dst, u_r[:, 2:2 + T], w[0], b if is_value else None, ALU.mult, ALU.add) if is_value
                         else ts(dst, u_r[:, 2:2 + T], w[0], None, ALU.mult))
                    link(stt(dst, u_r[:, 3:3 + T], w[1], dst, ALU.mult, ALU.add))
                    tail = u_r[:, LEAD + T - 72:].rearrange("p (a b) -> p a b", b=36)[:, :, 34:36]
                    out_ = st2[:, :, :].rearrange("p (a b) m -> p m a b", a=2)
                    step.on(nc.vector.tensor_copy(out_[:, bass.ds(it * 2 + m0, 1)][:, 0], tail))
                    stt(dst, u_r[:, 4:4 + T], w[2], dst, ALU.mult, ALU.add).then_inc(s_gc, 1)
            for m in range(KD):
                for q in range(3):
                    t = I_DOWN + 3 * m + q + 2
                    if t < N_ITEMS:
                        split_lo(t, t, min(KD, KF - KD * ((t - I_DOWN) % 3)) * P)
                dve.wait_ge(s_used, I_DOWN + 3 * (m + 1))
                if m >= 2:
                    dve.wait_ge(s_yt, m - 1)
                tt(halves(yT[:, m % 2, :]), pair(m), halves(xT[:, m, :]), ALU.add).then_inc(s_free, 1)

        @block.tensor
        def _(pe):
            mm = nc.tensor.matmul

            def product(x_h, x_l, rank, items, ready=None, midway=None):
                total = items[-1][2] + items[-1][3]
                for t, slot, k0, nk in items:
                    pe.wait_ge(s_lo, t + 1)
                    if ready is not None:
                        pe.wait_ge(ready[0], ready[1] + k0 + nk)
                    for k in range(nk):
                        if midway is not None and k == nk // 2:
                            midway()
                        cols = slice(k * P, (k + 1) * P)
                        for w, x, first in ((hi, x_h, True), (hi, x_l, False), (lo, x_h, False)):
                            for j in range(2):
                                last = mm(PS[:, 2 * rank + j, 0:HT], w[:, slot % 2, cols], x[:, k0 + k, j * HT:(j + 1) * HT],
                                          start=(k0 + k == 0 and first), stop=(k0 + k == total - 1 and w is lo))
                    last.then_inc(s_used, 1)

            def x_transpose(t):
                _, p0, n = TOK[t]
                pe.wait_ge(s_xt[t], 16)
                if t >= 2:
                    pe.wait_ge(s_xTa, t - 1)
                    pe.wait_ge(s_xTv, t - 1)
                for k in range(KD):
                    last = nc.tensor.transpose(PS[:, 2 * (t % 2) + k // 4, (k % 4) * P:(k % 4) * P + n],
                                               xnat[p0:, t, k * P:(k + 1) * P], ident[p0:, p0:])
                last.then_inc(s_xTd, 1)

            pe.wait_ge(s_ident, 16)
            for t in range(NTT):
                x_transpose(t)
            pe.wait_ge(s_rows, 16 * 14)
            for a, (c0, n) in enumerate(((0, V_N), (V_N, 2 * NU), (V_N + 2 * NU, 2 * NU), (V_N + 4 * NU, 2 * NU))):
                last = nc.tensor.transpose(PS[:, 6, c0:c0 + n], vrows[0:n, a, :], ident[0:n, 0:n])
            last.then_inc(s_vecT, 1)

            for t4 in range(4):
                pe.wait_ge(s_xl, 2 * t4 + 2)
                pe.wait_ge(s_lo, t4 + 1)
                for t, (c0, p0, n) in enumerate(TOK):
                    w0 = c0 - p0
                    for kk in range(2):
                        k = 2 * t4 + kk
                        cols = slice(kk * LAT, (kk + 1) * LAT)
                        for w, x in ((hi, xnh), (hi, xnl), (lo, xnh)):
                            last = mm(PS[:, 3 + t, 0:LAT], x[:, k, w0:w0 + P], w[:, t4 % 2, cols],
                                      start=(k == 0 and w is hi and x is xnh), stop=(k == KD - 1 and w is lo))
                last.then_inc(s_used, 1)
                if t4 == 2:
                    pe.wait_ge(s_rsn, 1)
                    for t, (c0, p0, n) in enumerate(TOK):
                        dst = PS[:, 0, c0:c0 + n] if t < NT else PS[:, 1, 0:n]
                        last = mm(dst, ones[:, :], dgx[:, t, p0:p0 + n], start=True, stop=True)
                    last.then_inc(s_rsb, 1)

            def products(it, g0, x_h, x_l, before=None, after=None):
                for r in range(4):
                    if before:
                        before(r)
                    pe.wait_ge(s_free, it * 4 + (g0 + r - 1) if g0 + r else it * 3)
                    product(x_h, x_l, r % 2, [(it * 4 + (I_IN + g0 + r), r, 0, KD)])
                    if after:
                        after(it, r)

            pe.wait_ge(s_rs, 1)
            pe.wait_ge(s_nat, 1)
            with pe.Fori(0, 2) as it:
                products(it, G_U, xnh, xnl)

            pe.wait_ge(s_nat, NTT)

            def lru(it, r):
                n = it * 4 + r
                pe.wait_ge(s_lw[r], it * 32 + 32)
                pe.wait_ge(s_uc, it * 4 + (r + 1))
                pe.wait_ge(s_lrui, n)
                for a in range(2):
                    for j in range(2):
                        last = mm(PS[:, 4 + 2 * a + j, 0:HT], lruw[:, r, a, :], one(uc, n, slice(j * HT, (j + 1) * HT))[:, 0],
                                  start=True, stop=True)
                last.then_inc(s_lru, 1)

            with pe.Fori(0, 2) as it:
                products(it, G_GA, xnh, xnl, after=lru)
            pe.wait_ge(s_state, 32)
            pe.wait_ge(s_free, G_GB - 1)
            for t in range(PAST // P):
                last = nc.tensor.transpose(PS[:, 0, t * P:(t + 1) * P], past[:, t, 0:P], ident[:, :])
            last.then_inc(s_lt, 1)
            for t in range(PAST // P):
                last = nc.tensor.transpose(PS[0:QK, 1, t * P:(t + 1) * P], past[:, t, KVL + ROPE - QK:], ident[:, :])
            last.then_inc(s_lt, 1)
            pe.wait_ge(s_nn, NTT)
            pe.wait_ge(s_krr, 2)
            pe.wait_ge(s_lrui, KD)
            for t, (c0, p0, n) in enumerate(TOK):
                if t == NT:
                    pe.wait_ge(s_free, G_GB)
                idn = ident[p0:, p0:]
                bank = PS[:, 4 + t if t < NT else 2, :]
                for a in range(3):
                    nc.tensor.transpose(bank[:, a * P:a * P + n], nat[p0:, t, a * P:(a + 1) * P], idn)
                nc.tensor.transpose(bank[0:QK, 3 * P:3 * P + n], nat[p0:, t, LAT - QK:LAT], idn).then_inc(s_lt, 1)
            pe.wait_ge(s_lte, 2)
            with pe.Fori(0, 2) as it:
                products(it, G_GB, xnh, xnl, before=lambda r: pe.wait_ge(s_lte, NTT + 2) if r == 1 else None)

            def keys_queries(q, par, u):
                if u == 0:
                    pe.wait_ge(s_wkq[par], q * 24 + (48 - 24 * par))
                    after(pe, s_vf, q * 3 - 3)
                    after(pe, s_kqf, q * 6)
                if u >= 2:
                    pe.wait_ge(s_kqf, q * 6 + (u - 1))
                bank = PS[:, u % 2, :]
                for a in range(TILES[u]):
                    if u < 3:
                        t = 4 * u + a
                        k0 = t * P if t < NKT - 1 else NK - P
                        last = mm(bank[:, a * P:(a + 1) * P], latT[:, k0:k0 + P], wkv[:, par, 0, :], start=True, stop=True)
                    else:
                        c0, p0, n = TOK[2 * (u - 3) + a]
                        for k in range(NQ):
                            last = mm(bank[:, a * 2 * QK:(a + 1) * 2 * QK], cqT[:, k, c0 - p0:c0 - p0 + P], wq[:, par, k, :],
                                      start=(k == 0), stop=(k == NQ - 1))
                last.then_inc(s_kq, 1)

            def transpose_kq(q, par, v, kq_before, v_before=None):
                bank = PS[:, v % 2, :]
                if v == 0:
                    pe.wait_ge(s_kqf, kq_before)
                    after(pe, s_vf, q * 3 if v_before is None else v_before)
                    pe.wait_ge(s_kn, q + 1)
                if v >= 2:
                    pe.wait_ge(s_trf, q * 5 + (v - 1))
                if v == 2:
                    pe.wait_ge(s_qr, q + 1)
                if v < 2:
                    for a in range(4):
                        last = nc.tensor.transpose(bank[:, a * P:(a + 1) * P],
                                                   Kn[:, par, 4 * v + a, :, :].rearrange("p h n -> p (h n)"), ident[:, :])
                elif v == 2:
                    nc.tensor.transpose(bank[:, 0:P], Kn[:, par, NKT - 1, :, :].rearrange("p h n -> p (h n)"), ident[:, :])
                    for h in range(2):
                        last = nc.tensor.transpose(bank[0:QK, P + h * DEC:P + (h + 1) * DEC], Qn[LASTP:, par, NT, h, :],
                                                   ident[LASTP:, LASTP:])
                else:
                    for a in range(4):
                        last = nc.tensor.transpose(bank[0:QK, a * P:(a + 1) * P], Qn[:, par, a, v - 3, :], ident[:, :])
                last.then_inc(s_tr, 1)

            def values_in(q, par, u):
                first = isinstance(q, int) and q == 0
                if u == 0:
                    pe.wait_ge(s_wv[par], q * 16 + (32 - 16 * par))
                if u < 2:
                    pe.wait_ge(s_kqf if first else s_trf, 12 if first else q * 5 + (4 + u))
                else:
                    pe.wait_ge(s_vf, q * 3 + 1)
                bank = PS[:, (u + 1) % 2, :]
                for a in range(TILES[u]):
                    t = 4 * u + a
                    k0 = t * P if t < NKT - 1 else NK - P
                    last = mm(bank[:, a * P:(a + 1) * P], latT[:, k0:k0 + P], wkv[:, par, 1, :], start=True, stop=True)
                last.then_inc(s_v, 1)

            def scores(p, par, n):
                h, t = divmod(n, 4)
                after(pe, s_e, p * 9 + (n - 2))
                bank = PS[:, SB[n % 3], :]
                if n == 0:
                    pe.wait_ge(s_trf, p * 5 + 5)
                if n < 8:
                    w = width(n)
                    mm(bank[:, 0:w], QT[0:QK + NT, 2 * par + h, t * P:(t + 1) * P], KT[0:QK + NT, 2 * par + h, 0:w],
                       start=True, stop=True).then_inc(s_s, 1)
                else:
                    for h in range(2):
                        q_s, k_s = QT[0:QK, 2 * par + h, S0:], KT[0:QK, 2 * par + h, :]
                        r0, r1 = slice(h * DEC, (h + 1) * DEC), slice((2 + h) * DEC, (3 + h) * DEC)
                        mm(bank[r0, 0:HP], q_s, k_s[:, SEQ:SEQ + HP], start=True, stop=True)
                        mm(bank[r1, 0:HP], q_s, k_s[:, SEQ + HP:SEQ + PAST], start=True, stop=True)
                        last = mm(bank[r0, HP:HP + DEC], q_s, k_s[:, SEQ + PAST:], start=True, stop=True)
                    last.then_inc(s_s, 1)

            def transpose_probs(p, par, n):
                pe.wait_ge(s_dg, p * 9 + (n + 1))
                after(pe, s_ptf, p * 9 + max(n - 1, 0))
                if n == 1:
                    after(pe, s_o, p * 2)
                bank = PS[:, 6 + (n + par) % 2, :]
                for a in range(n % 4 + 1 if n < 8 else 2):
                    last = mm(bank[:, a * P:(a + 1) * P], Pn[:, n % 3, a * P:(a + 1) * P], dg[:, n % 3, :], start=True, stop=True)
                if n == 8:
                    R2 = 2 * DEC
                    last = mm(bank[:, 2 * P:2 * P + R2], Pn[0:R2, 2, HP + DEC - P:HP + DEC], dg[0:R2, 2, 0:R2], start=True, stop=True)
                last.then_inc(s_pt, 1)

            def values(p, par, n):
                h, t = divmod(n, 4)
                b = (n + par) % 2
                pe.wait_ge(s_ptf, p * 9 + (n + 1))
                if n == 0:
                    pe.wait_ge(s_vf, p * 3 + 3)
                    after(pe, s_o, p * 2)
                if n < 8:
                    for a in range(t + 1):
                        last = mm(PS[h * VD:(h + 1) * VD, 3, t * P:(t + 1) * P], V[:, par, a, h, :], PT[:, b, a * P:(a + 1) * P],
                                  start=(a == 0), stop=(a == t))
                else:
                    for h in range(2):
                        dst = PS[h * VD:(h + 1) * VD, 6 + b, SEQ - DEC:SEQ]
                        for a in range(5):
                            c0 = (a % 2) * P + (a // 2) * 2 * DEC + h * DEC if a < 4 else 2 * P + h * DEC
                            last = mm(dst, V[:, par, 4 + a, h, :], PT[:, b, c0:c0 + DEC], start=(a == 0), stop=(a == 4))
                last.then_inc(s_pv, 1)

            def attend(p, par):
                kq = not isinstance(p, int) or p + 2 < NP_
                following = not isinstance(p, int) or p + 1 < NP_
                kq_before = p * 6 + 18 if kq else 6 * NP_
                for n in range(9):
                    if n < 7:
                        scores(p, par, n + 2)
                    elif following:
                        scores(p + 1, 1 - par, n - 7)
                    if kq and n < 3:
                        keys_queries(p + 2, par, 2 * n)
                        keys_queries(p + 2, par, 2 * n + 1)
                    if following:
                        for v in T_STEPS.get(n, ()):
                            transpose_kq(p + 1, 1 - par, v, kq_before)
                    transpose_probs(p, par, n)
                    if n:
                        values(p, par, n - 1)
                    if following and n == 6:
                        values_in(p + 1, 1 - par, 0)
                if following:
                    values_in(p + 1, 1 - par, 1)
                    values_in(p + 1, 1 - par, 2)
                values(p, par, 8)

            pe.wait_ge(s_free, G_OUT)
            pe.wait_ge(s_rope4, 48)
            for q in range(2):
                for u in range(6):
                    keys_queries(q, q, u)
            for u in range(3):
                values_in(0, 0, u)
            for v in range(5):
                transpose_kq(0, 0, v, 12, 3)
            pe.wait_ge(s_mask, 16 * 8)
            scores(0, 0, 0)
            scores(0, 0, 1)
            with pe.Fori(0, 3) as it:
                attend(it * 2, 0)
                attend(it * 2 + 1, 1)
            attend(6, 0)
            attend(7, 1)

            pe.wait_ge(s_ml, KD)
            with pe.Fori(0, 2) as it:
                products(it, G_OUT, mxh, mxl)
            nc.tensor.transpose(PS[0:64, 7, 0:P], st[:, :, :].rearrange("p a b -> p (a b)"), ident[:, :]).then_inc(s_stT, 1)

            def x2_sums():
                pe.wait_ge(s_ss2, KD)
                for j in range(2):
                    last = mm(PS[:, 4 + j, 0:HT], ones[:, :], x2ss[:, j * HT:(j + 1) * HT], start=True, stop=True)
                last.then_inc(s_x2t, 1)

            for r in range(4):
                pe.wait_ge(s_free, G_UP + r - 1)
                product(x2h, x2l, r % 2, [(I_UP + r, r, 0, KD)], (s_xl, KD) if r == 0 else None, x2_sums if r == 0 else None)
            with pe.Fori(1, NU // 4) as it:
                products(it, G_UP, x2h, x2l)

            def y_transpose(m):
                s = m % 2
                pe.wait_ge(s_free, G_DOWN + m + 1)
                if m >= 2:
                    pe.wait_ge(s_yn, 2 * m - 2)
                elif m == 1:
                    pe.wait_ge(s_stc, 2)
                for t, (c0, _, n) in enumerate(TOK):
                    dst = PS[0:n, 4 + 2 * s, t * P:(t + 1) * P] if t < NT else PS[0:n, 5 + 2 * s, 0:P]
                    last = nc.tensor.transpose(dst, yT[:, s, c0:c0 + n], ident[:, :])
                last.then_inc(s_yt, 1)

            for m in range(KD):
                items = [(I_DOWN + 3 * m + q, 3 * m + q, KD * q, min(KD, KF - KD * q)) for q in range(3)]
                pe.wait_ge(s_free, G_DOWN + m - 1)
                product(hh, hl, m % 2, items, (s_hl, 0) if m == 0 else None)
                if m == 0:
                    pe.wait_ge(s_gc, NU)
                    pe.wait_ge(s_stc, 1)
                    for a in range(2):
                        last = nc.tensor.transpose(PS[0:2 * NU, 7, a * P:(a + 1) * P],
                                                   st2[:, 2 * a:2 * a + 2, :].rearrange("p a b -> p (a b)"), ident[:, :])
                    last.then_inc(s_stT, 1)
                if m:
                    y_transpose(m - 1)
            y_transpose(KD - 1)


_INS = ["x_prompt", "x_sample", "cache_kv_latent", "cache_k_rope", "state_lru_h", "state_lru_conv", "state_ffn_conv",
        "g_mix_norm", "w_in", "g_q_a", "w_q_b", "g_kv_a", "w_kv_b", "g_qn", "g_qr", "g_kn", "g_kr",
        "lru_conv_w", "lru_conv_b", "w_rg", "b_rg", "w_ig", "b_ig", "lru_lambda", "w_out", "g_ffn_norm",
        "w_up", "ffn_conv_w", "ffn_conv_b", "w_down"]
_OUTS = [(1, SEQ, D), (1, DEC, D),
         (1, 1, SEQ, KVL), (1, 1, SEQ, ROPE), (1, 1, D), (1, 1, 3, D), (1, 1, 2, 2 * FF),
         (1, 1, DEC, KVL), (1, 1, DEC, ROPE), (1, 1, D), (1, 1, 3, D), (1, 1, 2, 2 * FF)]


def constants():
    inv = (THETA ** (-np.arange(0, ROPE, 2, dtype=np.float32) / ROPE)).astype(np.float32)
    rope = np.zeros((P, NTT, 2 * HR), np.float32)
    for t in range(NTT):
        pos = (np.arange(P) + t * P if t < NT else np.maximum(np.arange(P) - LASTP, 0) + PAST).astype(np.float32)
        ang = pos[:, None] * inv[None, :]
        rope[:, t, 0:HR], rope[:, t, HR:] = np.cos(ang), np.sin(ang)
    kmask, qmask = np.zeros((NT, NK), np.float32), np.zeros((NT, T), np.float32)
    for t in range(NT):
        kmask[t, t * P + CHUNK:(t + 1) * P] = MASKED
        qmask[t, t * P:t * P + CHUNK] = 1.0
    return {"ident": np.eye(P, dtype=np.float32), "rope": rope.reshape(P, -1), "kmask": kmask, "qmask": qmask}


def kernel(**inputs):
    import numpy as _np
    import concourse.bacc as _bacc
    from concourse import mybir as _mybir
    from concourse.bass_utils import run_bass_kernel_spmd as _run

    nc = _bacc.Bacc("TRN2", target_bir_lowering=False, num_devices=1)
    arrays, ins, consts, outs = {}, {}, {}, []
    for name in _INS:
        a = _np.ascontiguousarray(inputs[name])
        arrays[f"in_{name}_dram"] = a
        ins[name] = nc.dram_tensor(f"in_{name}_dram", a.shape, _mybir.dt.from_np(a.dtype), kind="ExternalInput").ap()
    for name, a in constants().items():
        arrays[f"const_{name}_dram"] = a
        consts[name] = nc.dram_tensor(f"const_{name}_dram", a.shape, _mybir.dt.from_np(a.dtype), kind="ExternalInput").ap()
    for n, shape in enumerate(_OUTS):
        outs.append(nc.dram_tensor(f"out_{n}_dram", shape, _mybir.dt.float32, kind="ExternalOutput").ap())
    layer(nc, ins, consts, outs)
    r = _run(nc, [arrays], core_ids=[0])
    return tuple(r.results[0][f"out_{n}_dram"] for n in range(len(_OUTS)))
```
